# Optimizing a Trainium2 kernel written in Bass

```python
import math
import jax
import jax.numpy as jnp
from jax import lax
import numpy as np

D_MODEL = 2048
BATCH = 1
SEQ = 256
DEPTH = 1

ALPHA = (2.0 * DEPTH) ** 0.25
BETA = (8.0 * DEPTH) ** -0.25
LN_EPS = 1e-5
RMS_EPS = 1e-6
HG_DK = 128
HG_DV = 128
HG_HEADS = D_MODEL // 128
HG_WIDTH = HG_HEADS * HG_DK
HG_CHUNK = 64
AT_DH = 128
AT_HEADS = D_MODEL // 128
AT_WIDTH = AT_HEADS * AT_DH
KV_RANK = D_MODEL // 8
IDX_HEADS = 16
IDX_DIM = 128
TOPK_MAX = 256
Q_BLOCK = 128
REL_BUCKETS = 32
REL_MAX_DIST = 128
MEM_LEN = 256
MEM_HEADS = 4
MEM_DH = D_MODEL // MEM_HEADS
PEER_HEADS = 8
PEER_NKEYS = 128
PEER_N = PEER_NKEYS * PEER_NKEYS
PEER_DKEY = 256
PEER_TOPK = 16
PEER_BLOCK = 128
IN_SIZES = (HG_WIDTH, HG_WIDTH, HG_WIDTH, HG_WIDTH, AT_WIDTH, KV_RANK, IDX_HEADS * IDX_DIM, IDX_DIM, IDX_HEADS, D_MODEL, D_MODEL)
IN_COLS = sum(IN_SIZES)

kernel_name = 'hgrn2_dsa_peer_gated_hybrid'

def layer_norm(x, g, b):
    xf = x.astype(jnp.float32)
    mu = jnp.mean(xf, axis=-1, keepdims=True)
    var = jnp.mean(jnp.square(xf - mu), axis=-1, keepdims=True)
    return ((xf - mu) * lax.rsqrt(var + LN_EPS) * g + b).astype(x.dtype)

def rms_norm(x, g):
    xf = x.astype(jnp.float32)
    return (xf * lax.rsqrt(jnp.mean(xf * xf, axis=-1, keepdims=True) + RMS_EPS) * g).astype(x.dtype)

def split_columns(t, sizes):
    idx, acc = [], 0
    for s in sizes[:-1]:
        acc += s
        idx.append(acc)
    return jnp.split(t, idx, axis=-1)

def t5_bucket(dist):
    max_exact = REL_BUCKETS // 2
    d = jnp.maximum(dist, 0)
    large = max_exact + (jnp.log(jnp.maximum(d, 1).astype(jnp.float32) / max_exact)
                         / math.log(REL_MAX_DIST / max_exact) * (REL_BUCKETS - max_exact)).astype(jnp.int32)
    large = jnp.minimum(large, REL_BUCKETS - 1)
    return jnp.where(d < max_exact, d, large)

def hgrn2_branch(q, f_raw, i, g_out, lb, norm_g):
    B, S, _ = q.shape
    C = HG_CHUNK
    N = S // C
    f = lb + (1.0 - lb) * jax.nn.sigmoid(f_raw.astype(jnp.float32))
    log_f = jnp.log(f)
    k = 1.0 - f

    def heads(t, d):
        return t.astype(jnp.float32).reshape(B, N, C, HG_HEADS, d).transpose(0, 3, 1, 2, 4)

    qh, kh, vh, gl = heads(q, HG_DK), heads(k, HG_DK), heads(i, HG_DV), heads(log_f, HG_DK)
    G = jnp.cumsum(gl, axis=3)
    G_last = G[:, :, :, -1:, :]
    G_ref = G[:, :, :, C // 2 - 1:C // 2, :]
    a = jnp.einsum('bhnik,bhnjk->bhnij', qh * jnp.exp(G - G_ref), kh * jnp.exp(G_ref - G))
    a = jnp.where(jnp.tril(jnp.ones((C, C), dtype=bool)), a, 0.0)
    o_intra = jnp.einsum('bhnij,bhnjv->bhniv', a, vh)
    q_dec = qh * jnp.exp(G)
    k_dec = kh * jnp.exp(G_last - G)
    chunk_decay = jnp.exp(G_last[:, :, :, 0, :])

    def step(state, xs):
        qd, kd, vc, dec = xs
        o = jnp.einsum('bhik,bhkv->bhiv', qd, state)
        state = dec[..., None] * state + jnp.einsum('bhjk,bhjv->bhkv', kd, vc)
        return state, o

    s0 = jnp.zeros((B, HG_HEADS, HG_DK, HG_DV), jnp.float32)
    mv = lambda t: jnp.moveaxis(t, 2, 0)
    _, o_inter = lax.scan(step, s0, (mv(q_dec), mv(k_dec), mv(vh), mv(chunk_decay)))
    o = o_intra + jnp.moveaxis(o_inter, 0, 2)
    o = o.transpose(0, 2, 3, 1, 4).reshape(B, S, HG_HEADS, HG_DV)
    o = rms_norm(o, norm_g.reshape(HG_HEADS, HG_DV).astype(jnp.float32))
    o = o.reshape(B, S, HG_WIDTH) * jax.nn.silu(g_out.astype(jnp.float32))
    return o.astype(q.dtype)

def dsa_branch(q, ckv, iq, ik, iw, kv_norm_g, ik_norm_g, ik_norm_b, w_uk, w_uv, rel_bias):
    B, S, _ = q.shape
    K = min(TOPK_MAX, S // 4)
    nb = S // Q_BLOCK
    ckv = rms_norm(ckv, kv_norm_g)
    ik = layer_norm(ik, ik_norm_g, ik_norm_b)
    q = q.reshape(B, S, AT_HEADS, AT_DH)
    q_lat = jnp.einsum('bshd,hrd->bshr', q, w_uk) * AT_DH ** -0.5
    iq = iq.reshape(B, S, IDX_HEADS, IDX_DIM)
    iw = iw * IDX_HEADS ** -0.5
    key_pos = jnp.arange(S, dtype=jnp.int32)

    def blocks(t):
        return jnp.moveaxis(t.reshape(B, nb, Q_BLOCK, *t.shape[2:]), 1, 0)

    def one_block(args):
        q_lat_b, iq_b, iw_b, start = args
        t_pos = start + jnp.arange(Q_BLOCK, dtype=jnp.int32)
        s_idx = jnp.einsum('bqhd,bsd->bqhs', iq_b, ik) * IDX_DIM ** -0.5
        score = jnp.einsum('bqhs,bqh->bqs', jax.nn.relu(s_idx), iw_b).astype(jnp.float32)
        score = jnp.where(key_pos[None, :] <= t_pos[:, None], score, -jnp.inf)
        _, sel = lax.top_k(score, K)
        valid = sel <= t_pos[None, :, None]
        c_sel = jax.vmap(lambda c, idx: c[idx])(ckv, sel)
        logits = jnp.einsum('bqhr,bqkr->bqhk', q_lat_b, c_sel).astype(jnp.float32)
        bias = rel_bias[t5_bucket(t_pos[None, :, None] - sel)]
        logits = logits + jnp.moveaxis(bias, -1, 2).astype(jnp.float32)
        logits = jnp.where(valid[:, :, None, :], logits, -jnp.inf)
        p = jax.nn.softmax(logits, axis=-1).astype(c_sel.dtype)
        o_lat = jnp.einsum('bqhk,bqkr->bqhr', p, c_sel)
        return jnp.einsum('bqhr,hrd->bqhd', o_lat, w_uv)

    starts = jnp.arange(nb, dtype=jnp.int32) * Q_BLOCK
    o = lax.map(one_block, (blocks(q_lat), blocks(iq), blocks(iw), starts))
    return jnp.moveaxis(o, 0, 1).reshape(B, S, AT_WIDTH)

def memory_cross_attention(x, mem, w_q, w_k, w_v, w_o):
    B, S, D = x.shape
    M = mem.shape[1]
    q = (x @ w_q).reshape(B, S, MEM_HEADS, MEM_DH)
    k = (mem @ w_k).reshape(B, M, MEM_HEADS, MEM_DH)
    v = (mem @ w_v).reshape(B, M, MEM_HEADS, MEM_DH)
    logits = jnp.einsum('bshd,bmhd->bhsm', q, k).astype(jnp.float32) * MEM_DH ** -0.5
    p = jax.nn.softmax(logits, axis=-1).astype(v.dtype)
    o = jnp.einsum('bhsm,bmhd->bshd', p, v).reshape(B, S, D)
    return o @ w_o

def peer_ffn(x, w_query, sub_keys, expert_u, expert_v):
    B, S, D = x.shape
    T = B * S
    xt = x.reshape(T, D)
    q = (xt @ w_query).reshape(T, PEER_HEADS, 2, PEER_DKEY // 2)
    s = jnp.einsum('thpd,hpnd->thpn', q, sub_keys).astype(jnp.float32)
    v_half, i_half = lax.top_k(s, PEER_TOPK)
    cand = v_half[:, :, 0, :, None] + v_half[:, :, 1, None, :]
    cand_idx = i_half[:, :, 0, :, None] * PEER_NKEYS + i_half[:, :, 1, None, :]
    top_s, top_pos = lax.top_k(cand.reshape(T, PEER_HEADS, -1), PEER_TOPK)
    experts = jnp.take_along_axis(cand_idx.reshape(T, PEER_HEADS, -1), top_pos, axis=-1)
    gate = jax.nn.softmax(top_s, axis=-1).astype(x.dtype)
    E = PEER_HEADS * PEER_TOPK
    nb = T // PEER_BLOCK

    def one_block(args):
        xb, eb, gb = args
        h = jax.nn.gelu(jnp.einsum('td,ted->te', xb, expert_u[eb]), approximate=False)
        return jnp.einsum('te,ted->td', gb * h, expert_v[eb])

    y = lax.map(one_block, (xt.reshape(nb, PEER_BLOCK, D), experts.reshape(nb, PEER_BLOCK, E),
                            gate.reshape(nb, PEER_BLOCK, E)))
    return y.reshape(B, S, D)

def setup_inputs(seed: int = 0) -> dict:
    key = jax.random.key(seed)
    ks = jax.random.split(key, 32)
    L, D = DEPTH, D_MODEL
    nrm = lambda k, shape, s: jax.random.normal(k, shape, jnp.float32) * s
    return {
        'x': nrm(ks[0], (BATCH, SEQ, D), 1.0),
        'mem': nrm(ks[1], (BATCH, MEM_LEN, D), 1.0),
        'w_in': nrm(ks[2], (L, D, IN_COLS), D ** -0.5),
        'lb_logits': nrm(ks[3], (L + 1, HG_WIDTH), 0.1),
        'hg_norm_g': 1.0 + nrm(ks[4], (L, HG_WIDTH), 0.02),
        'kv_norm_g': 1.0 + nrm(ks[5], (L, KV_RANK), 0.02),
        'ik_norm_g': 1.0 + nrm(ks[6], (L, IDX_DIM), 0.02),
        'ik_norm_b': nrm(ks[7], (L, IDX_DIM), 0.02),
        'w_uk': nrm(ks[8], (L, AT_HEADS, KV_RANK, AT_DH), KV_RANK ** -0.5),
        'w_uv': nrm(ks[9], (L, AT_HEADS, KV_RANK, AT_DH), KV_RANK ** -0.5 * BETA),
        'rel_bias': nrm(ks[10], (REL_BUCKETS, AT_HEADS), 0.5),
        'w_branch_a': nrm(ks[11], (L, HG_WIDTH, D), HG_WIDTH ** -0.5 * BETA),
        'w_branch_b': nrm(ks[12], (L, AT_WIDTH, D), AT_WIDTH ** -0.5 * BETA),
        'w_mix_out': nrm(ks[13], (L, D, D), D ** -0.5 * BETA),
        'ln1_g': 1.0 + nrm(ks[14], (L, D), 0.02),
        'ln1_b': nrm(ks[15], (L, D), 0.02),
        'w_cq': nrm(ks[16], (L, D, D), D ** -0.5),
        'w_ck': nrm(ks[17], (L, D, D), D ** -0.5),
        'w_cv': nrm(ks[18], (L, D, D), D ** -0.5 * BETA),
        'w_co': nrm(ks[19], (L, D, D), D ** -0.5 * BETA),
        'ln2_g': 1.0 + nrm(ks[20], (L, D), 0.02),
        'ln2_b': nrm(ks[21], (L, D), 0.02),
        'w_pq': nrm(ks[22], (L, D, PEER_HEADS * PEER_DKEY), D ** -0.5),
        'peer_keys': nrm(ks[23], (L, PEER_HEADS, 2, PEER_NKEYS, PEER_DKEY // 2), (PEER_DKEY // 2) ** -0.5),
        'peer_u': nrm(ks[24], (L, PEER_N, D), D ** -0.5),
        'peer_v': nrm(ks[25], (L, PEER_N, D), BETA),
        'ln3_g': 1.0 + nrm(ks[26], (L, D), 0.02),
        'ln3_b': nrm(ks[27], (L, D), 0.02),
    }

def reference(x, mem, w_in, lb_logits, hg_norm_g, kv_norm_g, ik_norm_g, ik_norm_b, w_uk, w_uv,
              rel_bias, w_branch_a, w_branch_b, w_mix_out, ln1_g, ln1_b, w_cq, w_ck, w_cv, w_co,
              ln2_g, ln2_b, w_pq, peer_keys, peer_u, peer_v, ln3_g, ln3_b):
    lower_bounds = jnp.cumsum(jax.nn.softmax(lb_logits.astype(jnp.float32), axis=0), axis=0)
    h = x
    for l in range(DEPTH):
        proj = h @ w_in[l]
        hq, hf, hi, hg, aq, ackv, aiq, aik, aiw, gate_a, gate_b = split_columns(proj, IN_SIZES)
        ya = hgrn2_branch(hq, hf, hi, hg, lower_bounds[l], hg_norm_g[l]) @ w_branch_a[l]
        yb = dsa_branch(aq, ackv, aiq, aik, aiw, kv_norm_g[l], ik_norm_g[l], ik_norm_b[l],
                        w_uk[l], w_uv[l], rel_bias) @ w_branch_b[l]
        mix = (jax.nn.sigmoid(gate_a) * ya + jax.nn.sigmoid(gate_b) * yb) @ w_mix_out[l]
        h = layer_norm(ALPHA * h + mix, ln1_g[l], ln1_b[l])
        ca = memory_cross_attention(h, mem, w_cq[l], w_ck[l], w_cv[l], w_co[l])
        h = layer_norm(ALPHA * h + ca, ln2_g[l], ln2_b[l])
        ff = peer_ffn(h, w_pq[l], peer_keys[l], peer_u[l], peer_v[l])
        h = layer_norm(ALPHA * h + ff, ln3_g[l], ln3_b[l])
    return h


_drawn_inputs = setup_inputs


def setup_inputs(seed=0):
    import zlib

    import numpy as np

    out = dict(_drawn_inputs(seed))
    spreads = {}
    factors = {'hg_norm_g': 5.447,
     'kv_norm_g': 8.0,
     'ik_norm_g': 5.139,
     'ik_norm_b': 6.561,
     'ln3_g': 2.897,
     'ln3_b': 2.826}
    for name, (base, spread) in spreads.items():
        noise = np.random.default_rng([zlib.crc32(name.encode()), seed]).standard_normal(out[name].shape)
        drawn = base * np.exp(spread * noise) if base else spread * noise
        out[name] = jnp.asarray(drawn.astype(out[name].dtype))
    for name, factor in factors.items():
        out[name] = (out[name] * factor).astype(out[name].dtype)
    return out
```

```python
import math
from contextlib import ExitStack

import numpy as np

import concourse.bass as bass
from concourse import mybir

F32 = mybir.dt.float32
U32 = mybir.dt.uint32
ALU = mybir.AluOpType
ACT = mybir.ActivationFunctionType
AX = mybir.AxisListType

P = 128
D = 2048
SEQ = 256
TB = SEQ // P
KT = D // P
UN = 256
UPM = D // UN
DEPTH = 1
ALPHA = (2.0 * DEPTH) ** 0.25
LN_EPS = 1e-5
RMS_EPS = 1e-6
HEADS = 16
PAIRS = HEADS // 2
CHUNK = 64
NCH = SEQ // CHUNK
AT_DH = 128
IDX_DIM = 128
TOPK = min(256, SEQ // 4)
REL_BUCKETS = 32
REL_MAX_DIST = 128
MEM_HEADS = 4
MEM_DH = D // MEM_HEADS
PEER_HEADS = 8
NKEYS = 128
PK = 16
NE = PEER_HEADS * PK
BATCH = 4
BPB = NE // BATCH
PIECES = 4
EARLY = 2 * (PEER_HEADS - 1)
MASKED = -1e30
TAKEN = -3e38

C_HQ, C_HF, C_HI, C_HG, C_AQ = 0, D, 2 * D, 3 * D, 4 * D
C_CKV = 5 * D
C_IQ = C_CKV + 256
C_IK = C_IQ + D
C_GA = C_IK + IDX_DIM + HEADS
C_GB = C_GA + D

U_CKV, U_IK = 0, 1
U_HG = 2
U_CK = U_HG + 4 * PAIRS
U_IQ = U_CK + UPM
U_GA = U_IQ + UPM
U_AQ = U_GA + 2 * UPM
U_WB = U_AQ + 2 * UPM
U_MIX = U_WB + UPM
U_CV = U_MIX + UPM
U_CQ = U_CV + UPM
U_CO = U_CQ + UPM
U_PQ = U_CO + UPM
UNITS = U_PQ + UPM

K_ID, K_MEAN, K_AMASK, K_RESET, K_CAUS, K_IOTA = 0, 128, 256, 384, 896, 1280
K_ALPHA = 1296
K_END = 1424


def constants():
    c = np.zeros((P, K_END), np.float32)
    i = np.arange(P)
    c[:, K_ID:K_ID + P] = np.eye(P)
    c[:, K_MEAN:K_MEAN + P] = 1.0 / P
    c[:, K_AMASK:K_AMASK + P] = (i[:, None] <= i[None, :]) & (i[:, None] // CHUNK == i[None, :] // CHUNK)
    c[:, K_RESET:K_RESET + 512] = (np.arange(512) % CHUNK != 0)[None, :]
    c[:, K_CAUS:K_CAUS + 256] = np.where(np.arange(256)[None, :] <= P + i[:, None], 0.0, MASKED)
    c[:, K_CAUS + 256:K_CAUS + 384] = np.where(i[None, :] <= i[:, None], 0.0, MASKED)
    c[:, K_IOTA:K_IOTA + PK] = np.arange(PK)[None, :]
    c[:, K_ALPHA:K_ALPHA + P] = np.eye(P) * ALPHA
    return c


def bucket_hits():
    dist = np.maximum(255 - np.arange(384), 0)
    exact = REL_BUCKETS // 2
    large = exact + (np.log(np.maximum(dist, 1) / exact) / math.log(REL_MAX_DIST / exact) * (REL_BUCKETS - exact)).astype(np.int64)
    bucket = np.where(dist < exact, dist, np.minimum(large, REL_BUCKETS - 1))
    return (bucket[None, :] == np.arange(REL_BUCKETS)[:, None]).astype(np.float32)


class Chain:

    def __init__(self, eng, sem):
        self.eng, self.sem, self.base, self.k = eng, sem, 0, 0

    def link(self, ins):
        ins.then_inc(self.sem, 1)
        self.k += 1
        self.eng.wait_ge(self.sem, self.base + self.k)

    def loop(self, i, per):
        self.outer = self.base + self.k
        self.base, self.k, self.per = self.outer + i * per, 0, per

    def end(self, times):
        assert self.k == self.per, (self.k, self.per)
        self.base, self.k = self.outer + times * self.per, 0


def trunk_layer(nc, x_tok, x_cols, mem_cols, units, const, hits, rel_bias, lb_logits, hg_norm, kv_g, ik_g, ik_b,
                w_ukv, keys_cols, ln_rows, peer_u, peer_v, rb_scratch, out, dbg=None):
    with ExitStack() as ctx:
        def sem(name):
            return ctx.enter_context(nc.semaphore(name))

        arena = ctx.enter_context(nc.sbuf_tensor("arena", [P, 52900], F32))
        top = [0]

        def take(n):
            top[0] += n
            assert top[0] <= 52900
            return arena[:, top[0] - n:top[0]]

        def inside(region, at, n):
            return region[:, at:at + n]

        w_ring = take(4 * 4096)
        W = [inside(w_ring, 4096 * s, 4096) for s in range(4)]
        R_X, R_O, R_M, R_B, R_K = (take(4096) for _ in range(5))
        R_S = take(13312)
        C = take(K_END)
        ckv_t = take(512)
        ik_t = take(256)
        iw = take(32)
        small = take(192)
        stats = take(96)
        idx_fix = take(2 * BATCH).bitcast(U32)
        xt = R_X
        h_tok = R_X
        oh = R_O
        gate_b = R_O
        h_t = R_O
        mem_a = R_M
        mix_t = R_M
        oc_t = R_M
        ckv = inside(R_B, 0, 512)
        ikw = inside(R_B, 512, 512)
        cn = inside(R_B, 1024, 512)
        row_kv = inside(R_B, 1536, 256)
        row_ikg = inside(R_B, 1792, 128)
        row_ikb = inside(R_B, 1920, 128)
        iq = [inside(R_B, 2048 + 512 * n, 512) for n in range(2)]
        relu = [inside(R_B, 768 * n, 768) for n in range(2)]
        score = inside(R_B, 3072, 384)
        ob_t = R_B
        mem_b = R_B
        kc_t = R_K
        at = [0]

        def part(n):
            at[0] += n
            assert at[0] <= 13312
            return inside(R_S, at[0] - n, n)

        a_sf, a_q, a_v, a_sg, a_gr, a_f, a_k, a_g, a_gd, a_gl, a_t2, a_sq = (part(512) for _ in range(12))
        a_ex, a_pr = part(2048), part(2048)
        a_kd, a_at = part(512), part(512)
        a_st = part(768)
        at[0] = 0
        th = part(HEADS * 256)
        wukv = [part(1024) for _ in range(2)]
        aq = [part(512) for _ in range(2)]
        khs, vhs = part(512), part(512)
        lg, pt = part(768), part(768)
        sel_mask = part(384)
        biases = part(768)
        ga = [part(512) for _ in range(2)]
        yb = [part(512) for _ in range(2)]
        at[0] = 0
        vc = part(4096)
        ln_g, ln_b = part(D), part(D)
        qc = [part(1024) for _ in range(2)]
        pc, ptc = part(512), part(512)
        yz = [part(512) for _ in range(2)]
        at[0] = 8192
        qp = part(512)
        sc, sc2 = part(512), part(512)
        cand = part(512)
        eq = part(512)
        gates = part(TB * NE)
        experts = part(TB * NE).bitcast(U32)
        v16 = part(64)
        i16 = part(64).bitcast(U32)
        i16f = part(64)
        top_s, e_top = part(32), part(32)
        pos = part(32).bitcast(U32)
        posh = part(64).bitcast(U32)
        poshf = part(64)
        idxh = part(64)
        dots, hg4, gh4 = part(BATCH), part(BATCH), part(BATCH)
        diag = part(BATCH * P)
        keys_t = inside(R_K, 0, 2048)
        u_rows = [inside(R_M, 0, D), inside(R_M, D, D), inside(R_B, 0, D), inside(R_B, D, D)]
        v_rows = [inside(R_S, D * n, D) for n in range(4)]
        fin_g, fin_b = inside(w_ring, 0, D), inside(w_ring, D, D)
        fin_x = inside(w_ring, 2 * D, D)

        ident, mean_m = inside(C, K_ID, P), inside(C, K_MEAN, P)
        lbr = inside(small, 0, 32)
        lb = inside(small, 32, 16)
        omlb = inside(small, 48, 16)
        hgn = inside(small, 64, 16)
        lbm = inside(small, 80, 16)
        ss, rs = inside(small, 96, 2), inside(small, 98, 2)
        mv = inside(small, 100, 4)
        m8 = inside(small, 104, 8)
        nmax, esum, rec = inside(small, 112, 4), inside(small, 116, 4), inside(small, 120, 4)
        eps_ln, eps_rms = inside(small, 124, 1), inside(small, 125, 1)
        g2 = inside(small, 126, 2)
        nmax2 = inside(small, 128, 4)

        PS = ctx.enter_context(nc.psum_tensor("PS", [P, 8, 512], F32))
        PJ = [PS[:, b, :] for b in range(4)]
        B = [PS[:, 4 + b, :] for b in range(4)]
        B01, B23 = PS[:, 4:6, :], PS[:, 6:8, :]

        def update(c, h):
            return B[3][:, h * P:(h + 1) * P] if c == 1 else B[2][:, (c + h) * P:(c + h + 1) * P]

        w_landed = [sem(f"w_landed{s}") for s in range(4)]
        proj_done = sem("proj_done")
        evac_done = sem("evac_done")
        act_chain, dve_chain = sem("act_chain"), sem("dve_chain")
        const_in, mem_in, row_in, rb_in, rb_out = (sem(n) for n in ("const_in", "mem_in", "row_in", "rb_in", "rb_out"))
        x_in = [sem(f"x_in{n}") for n in range(PIECES)]
        w0_in = [sem(f"w0_in{n}") for n in range(PIECES - 1)]
        th_in, xtok_in = sem("th_in"), sem("xtok_in")
        ukv_in = [sem(f"ukv_in{n}") for n in range(2)]
        keys_in, ln_in, fin_in, out_done = sem("keys_in"), sem("ln_in"), sem("fin_in"), sem("out_done")
        f_ready, lf_ready, g_ready, ex_ready, qk_ready = (sem(n) for n in ("f_ready", "lf_ready", "g_ready", "ex_ready", "qk_ready"))
        kd_ps, kd_sb, at_ps, at_sb, u_ps, st_sb, ot_ps, sq_sb, ms_ps, rs_sb, t2_done, gate_rd, oh_done = (
            sem(n) for n in ("kd_ps", "kd_sb", "at_ps", "at_sb", "u_ps", "st_sb", "ot_ps", "sq_sb", "ms_ps", "rs_sb",
                             "t2_done", "gate_rd", "oh_done"))
        ss_done, mv_done, rn_done, cn_done, cn_ps, cn_sb, lb_done, eps_set, rb_ps = (
            sem(n) for n in ("ss_done", "mv_done", "rn_done", "cn_done", "cn_ps", "cn_sb", "lb_done", "eps_set", "rb_ps"))
        rb_sb = sem("rb_sb")
        lbe_done, lbd_done = sem("lbe_done"), sem("lbd_done")
        sidx_ps, relu_sb, acc_done = sem("sidx_ps"), sem("relu_sb"), sem("acc_done")
        sel_done = sem("sel_done")
        mixa_done, mixb_done = sem("mixa_done"), sem("mixb_done")
        kv_ps, kv_sb, lg_ps, lg_rd, p_exp, p_ready, pt_ps, pt_sb, ob_ps, ob_sb = (
            sem(n) for n in ("kv_ps", "kv_sb", "lg_ps", "lg_rd", "p_exp", "p_ready", "pt_ps", "pt_sb", "ob_ps", "ob_sb"))
        z_done, lnv_done, lnr_done, h_done, tr_ps, tr_sb = (
            sem(n) for n in ("z_done", "lnv_done", "lnr_done", "h_done", "tr_ps", "tr_sb"))
        cl_ps, cl_rd, ce_done, cp_done, ct_ps, ct_sb, co_ps, co_sb = (
            sem(n) for n in ("cl_ps", "cl_rd", "ce_done", "cp_done", "ct_ps", "ct_sb", "co_ps", "co_sb"))
        psc_ps, psc_sb, tops_rd, gexp_done, head_done = (
            sem(n) for n in ("psc_ps", "psc_sb", "tops_rd", "gexp_done", "head_done"))
        idx_set = sem("idx_set")
        u_in = [sem(f"u_in{n}") for n in range(BATCH)]
        v_in = [sem(f"v_in{n}") for n in range(BATCH)]
        dot_done, gh_done, diag_done, v_used = sem("dot_done"), sem("gh_done"), sem("diag_done"), sem("v_used")
        fin_done = sem("fin_done")
        u_slot_free, v_slot_free, idx_seen, at_seen, max_seen = (
            sem(n) for n in ("u_slot_free", "v_slot_free", "idx_seen", "at_seen", "max_seen"))

        block = ctx.enter_context(nc.Block())

        @block.sync
        def _(sp):
            for n in range(PIECES):
                cols = slice(n * 4096 // PIECES, (n + 1) * 4096 // PIECES)
                sp.dma_start(xt[:, cols], x_cols[:, cols]).then_inc(x_in[n], 16)
                sp.dma_start(W[0][:, cols], units[0][:, cols]).then_inc(w_landed[0] if n == PIECES - 1 else w0_in[n], 16)
            for u in range(1, 4):
                sp.dma_start(W[u], units[u]).then_inc(w_landed[u], 16)
                if u == 1:
                    sp.dma_start(C, const).then_inc(const_in, 16)
            whole = (UNITS - 4) // 4
            with sp.Fori(0, whole) as i:
                for s in range(4):
                    sp.wait_ge(proj_done, i * 4 + s + 1)
                    sp.dma_start(W[s], units[bass.ds(i * 4 + s + 4, 1)].rearrange("a p n -> (a p) n")).then_inc(w_landed[s], 16)
            for u in range(4 + 4 * whole, UNITS):
                sp.wait_ge(proj_done, u - 3)
                sp.dma_start(W[u % 4], units[u]).then_inc(w_landed[u % 4], 16)
            sp.wait_ge(proj_done, UNITS)
            sp.dma_start(fin_g, ln_rows[4].partition_broadcast(P)).then_inc(fin_in, 16)
            sp.dma_start(fin_b, ln_rows[5].partition_broadcast(P)).then_inc(fin_in, 16)
            for tb in range(TB):
                sp.wait_ge(fin_done, tb + 1)
                sp.dma_start(out[tb], fin_x).then_inc(out_done, 16)
            sp.wait_ge(out_done, 16 * TB)

        @block.gpsimd
        def _(pool):
            nc.gpsimd.memset(eps_ln, LN_EPS).then_inc(eps_set, 1)
            nc.gpsimd.memset(eps_rms, RMS_EPS).then_inc(eps_set, 1)
            pool.dma_start(lbr, lb_logits).then_inc(row_in, 16)
            pool.dma_start(hgn, hg_norm).then_inc(row_in, 16)
            pool.dma_start(row_kv, kv_g.partition_broadcast(P)).then_inc(row_in, 16)
            pool.dma_start(row_ikg, ik_g.partition_broadcast(P)).then_inc(row_in, 16)
            pool.dma_start(row_ikb, ik_b.partition_broadcast(P)).then_inc(row_in, 16)
            pool.dma_start(oh[0:32, 0:384], hits).then_inc(rb_in, 16)
            pool.dma_start(oh[0:32, 384:400], rel_bias).then_inc(rb_in, 16)
            pool.wait_ge(rb_sb, 1)
            pool.dma_start(rb_scratch, oh[0:16, 512:896].unsqueeze(1).to_broadcast([16, P, 384])).then_inc(rb_out, 16)
            pool.dma_start(mem_a, mem_cols).then_inc(mem_in, 16)
            pool.wait_ge(rb_out, 16)
            pool.wait_ge(oh_done, 2 * PAIRS)
            pool.dma_start(th.rearrange("p (h x) -> p h x", h=HEADS),
                           bass.AP(rb_scratch.tensor, 127, [[383, P], [P * 384, HEADS], [1, 256]])).then_inc(th_in, 16)
            for j in range(PAIRS):
                if j >= 2:
                    pool.wait_ge(kv_ps, j - 1)
                pool.dma_start(wukv[j % 2], w_ukv[j]).then_inc(ukv_in[j % 2], 16)
            pool.wait_ge(proj_done, U_WB)
            pool.dma_start(h_tok, x_tok).then_inc(xtok_in, 16)
            pool.wait_ge(proj_done, U_MIX)
            pool.dma_start(mem_b, mem_cols).then_inc(mem_in, 16)
            for n in range(2):
                if n:
                    pool.wait_ge(h_done, 2)
                else:
                    pool.wait_ge(mixb_done, UPM + 2)
                pool.dma_start(ln_g, ln_rows[2 * n].partition_broadcast(P)).then_inc(ln_in, 16)
                pool.dma_start(ln_b, ln_rows[2 * n + 1].partition_broadcast(P)).then_inc(ln_in, 16)
            pool.wait_ge(cl_ps, MEM_HEADS)
            pool.dma_start(keys_t, keys_cols).then_inc(keys_in, 16)
            pool.wait_ge(proj_done, U_PQ)
            pool.wait_ge(h_done, 4)

            def gather(b, par):
                first = isinstance(b, int) and b == 0
                pool.wait_ge(idx_set, b + 1)
                pool.sem_inc(idx_seen, 1)
                for e in range(BATCH):
                    if not first:
                        pool.wait_ge(dot_done, BATCH * (b - 1) + e + 1)
                        pool.sem_inc(u_slot_free, 1)
                    nc.gpsimd.indirect_dma_start(
                        out=u_rows[e], out_offset=None, in_=peer_u,
                        in_offset=bass.IndirectOffsetOnAxis(ap=idx_fix[:, par * BATCH + e:par * BATCH + e + 1], axis=0),
                    ).then_inc(u_in[e], 16)
                for e in range(BATCH):
                    if not first:
                        pool.wait_ge(v_used, BATCH * (b - 1) + e + 1)
                        pool.sem_inc(v_slot_free, 1)
                    nc.gpsimd.indirect_dma_start(
                        out=v_rows[e], out_offset=None, in_=peer_v,
                        in_offset=bass.IndirectOffsetOnAxis(ap=idx_fix[:, par * BATCH + e:par * BATCH + e + 1], axis=0),
                    ).then_inc(v_in[e], 16)

            gather(0, 0)
            gather(1, 1)
            with pool.Fori(1, TB * BPB // 2) as i:
                for par in range(2):
                    gather(i * 2 + par, par)

        @block.tensor
        def _(pe):
            mm = nc.tensor.matmul

            def unit(i, c, rows, act_t, halves=(0, 1), bank=None):
                slot = c % 4
                bank = PJ[slot] if bank is None else bank
                for n in halves:
                    first = isinstance(i, int) and 4 * i + c == 0
                    if n == 0 and not first:
                        pe.wait_ge(w_landed[slot], i * 16 + 16 * (c // 4 + 1))
                        if not (isinstance(i, int) and 4 * i + c < 4):
                            pe.wait_ge(evac_done, i * 4 + c - 3)
                    for k in range(KT):
                        if first and n == 0 and k % (KT // PIECES) == 0:
                            piece = k // (KT // PIECES)
                            pe.wait_ge(x_in[piece], 16)
                            pe.wait_ge(w_landed[0] if piece == PIECES - 1 else w0_in[piece], 16)
                        if rows:
                            lhs = act_t[:, k * SEQ + n * P:k * SEQ + n * P + P]
                            rhs = W[slot][:, k * UN:(k + 1) * UN]
                        else:
                            lhs = W[slot][:, k * UN + n * P:k * UN + n * P + P]
                            rhs = act_t[:, k * SEQ:(k + 1) * SEQ]
                        ins = mm(bank[:, n * 256:(n + 1) * 256], lhs, rhs, start=k == 0, stop=k == KT - 1)
                    if n == 1:
                        ins.then_inc(proj_done, 1)

            def transpose(dst, src):
                return nc.tensor.transpose(dst, src, ident)

            unit(0, U_CKV, True, xt)
            pe.wait_ge(rb_in, 32)
            mm(B[3][0:16, 0:384], oh[0:32, 384:400], oh[0:32, 0:384], start=True, stop=True).then_inc(rb_ps, 1)
            unit(0, U_IK, True, xt)
            pe.wait_ge(const_in, 16)

            def hg_scores(p):
                pe.wait_ge(qk_ready, p * 4 + 4)
                for g in range(4):
                    ins = transpose(B[0][:, g * P:(g + 1) * P], a_pr[:, 1536 + g * P:1536 + (g + 1) * P])
                ins.then_inc(kd_ps, 1)
                for g in range(4):
                    ins = mm(B[1][:, g * P:(g + 1) * P], a_pr[:, 512 + g * P:512 + (g + 1) * P], a_pr[:, g * P:(g + 1) * P],
                             start=True, stop=True)
                ins.then_inc(at_ps, 1)

            def hg_updates(p):
                pe.wait_ge(kd_sb, p + 1)
                pe.wait_ge(evac_done, p * 4 + U_HG + 3)
                for h in range(2):
                    for c in range(NCH - 1):
                        g, r = h * 2 + c // 2, (c % 2) * CHUNK
                        ins = mm(update(c, h), a_kd[r:r + CHUNK, g * P:(g + 1) * P],
                                 a_v[r:r + CHUNK, (c // 2) * 256 + h * P:(c // 2) * 256 + (h + 1) * P], start=True, stop=True)
                ins.then_inc(u_ps, 1)

            def hg_out(p):
                pe.wait_ge(at_sb, p + 1)
                pe.wait_ge(st_sb, p + 1)
                for h in range(2):
                    for tb in range(TB):
                        o = h * 256 + tb * P
                        ins = mm(B[0][:, o:o + P], a_v[:, tb * 256 + h * P:tb * 256 + (h + 1) * P],
                                 a_at[:, (h * 2 + tb) * P:(h * 2 + tb + 1) * P], start=True, stop=True, skip_group_check=True)
                        for c in (2 * tb, 2 * tb + 1):
                            if c:
                                o = h * 256 + c * CHUNK
                                ins = mm(B[0][:, o:o + CHUNK], a_st[:, h * 384 + (c - 1) * P:h * 384 + c * P],
                                         a_pr[:, 1024 + o:1024 + o + CHUNK], start=False, stop=True, skip_group_check=True)
                ins.then_inc(ot_ps, 1)

            def hg_mean(p):
                pe.wait_ge(sq_sb, p + 1)
                mm(B[1], mean_m, a_sq, start=True, stop=True).then_inc(ms_ps, 1)

            hg_steps = (hg_scores, hg_updates, hg_out, hg_mean)

            def hg_body(p):
                for n in range(4):
                    rows = n == 2
                    unit(p, U_HG + n, rows, xt)
                    hg_steps[n](p - 1)

            for n in range(3):
                unit(0, U_HG + n, n == 2, xt)
            pe.wait_ge(cn_done, 4)
            for rc in range(2):
                for tb in range(TB):
                    transpose(B[0][:, rc * 256 + tb * P:rc * 256 + (tb + 1) * P], cn[:, tb * 256 + rc * P:tb * 256 + (rc + 1) * P])
            for tb in range(TB):
                ins = transpose(B[1][:, tb * P:(tb + 1) * P], ikw[:, tb * 256:tb * 256 + P])
            ins.then_inc(cn_ps, 1)
            unit(0, U_HG + 3, False, xt)
            pe.wait_ge(cn_sb, 2)
            with pe.Fori(1, PAIRS) as p:
                hg_body(p)

            pe.wait_ge(mem_in, 16)
            for j in range(UPM):
                unit(8, U_CK - 32 + j, False, mem_a)
                if j < 4:
                    hg_steps[j](PAIRS - 1)

            def index_scores(j):
                pe.wait_ge(evac_done, U_IQ + j + 1)
                if j >= 2:
                    pe.wait_ge(relu_sb, j - 1)
                elif j == 0:
                    pe.wait_ge(oh_done, 2 * PAIRS)
                for h in range(2):
                    bank = B[2 * (j % 2) + h]
                    q = iq[j % 2][:, h * 256:(h + 1) * 256]
                    mm(bank[:, 0:256], q[:, P:256], ik_t, start=True, stop=True)
                    ins = mm(bank[:, 256:384], q[:, 0:P], ik_t[:, 0:P], start=True, stop=True)
                ins.then_inc(sidx_ps, 1)

            for j in range(UPM):
                unit(0, U_IQ + j, False, xt)
                if j:
                    index_scores(j - 1)
            index_scores(UPM - 1)

            with pe.Fori(0, UPM // 2) as it:
                for n in range(4):
                    unit(it + U_GA // 4, U_GA % 4 + n, False, xt if n % 2 == 0 else oh)

            def keys_values(j, par, turn):
                pe.wait_ge(ukv_in[par], turn * 16 + 16)
                if isinstance(j, int) and j == 0:
                    pe.wait_ge(relu_sb, UPM)
                else:
                    pe.wait_ge(ob_sb, j)
                    pe.wait_ge(kv_sb, j * 2)
                for h in range(2):
                    for rc in range(2):
                        mm(B[0][:, h * 256:(h + 1) * 256], wukv[par][:, rc * 256 + h * P:rc * 256 + (h + 1) * P],
                           ckv_t[:, rc * 256:(rc + 1) * 256], start=rc == 0, stop=rc == 1)
                for sb in range(TB):
                    for rc in range(2):
                        ins = mm(B[1][:, sb * 256:(sb + 1) * 256], ckv_t[:, rc * 256 + sb * P:rc * 256 + (sb + 1) * P],
                                 wukv[par][:, 512 + rc * 256:512 + (rc + 1) * 256], start=rc == 0, stop=rc == 1)
                ins.then_inc(kv_ps, 1)

            def logits(j, par):
                pe.wait_ge(kv_sb, j * 2 + 2)
                pe.wait_ge(evac_done, j * 2 + U_AQ + 1)
                if not (isinstance(j, int) and j == 0):
                    pe.wait_ge(pt_sb, j)
                for h in range(2):
                    q = aq[par][:, h * 256:(h + 1) * 256]
                    mm(B[2 + h][:, 0:256], q[:, P:256], khs[:, h * 256:(h + 1) * 256], start=True, stop=True)
                    ins = mm(B[2 + h][:, 256:384], q[:, 0:P], khs[:, h * 256:h * 256 + P], start=True, stop=True)
                ins.then_inc(lg_ps, 1)

            def turn_probs(j):
                pe.wait_ge(p_ready, j * 2 + 2)
                for h in range(2):
                    for c in range(3):
                        ins = transpose(B[2 + h][:, c * P:(c + 1) * P], lg[:, h * 384 + c * P:h * 384 + (c + 1) * P])
                ins.then_inc(pt_ps, 1)

            def attend(j):
                pe.wait_ge(pt_sb, j + 1)
                for h in range(2):
                    v = [vhs[:, sb * 256 + h * P:sb * 256 + (h + 1) * P] for sb in range(TB)]
                    pr = pt[:, h * 384:(h + 1) * 384]
                    mm(B[0][:, h * 256:h * 256 + P], v[0], pr[:, 256:384], start=True, stop=True)
                    mm(B[0][:, h * 256 + P:(h + 1) * 256], v[0], pr[:, 0:P], start=True, stop=False)
                    ins = mm(B[0][:, h * 256 + P:(h + 1) * 256], v[1], pr[:, P:256], start=False, stop=True)
                ins.then_inc(ob_ps, 1)

            def sparse_body(i, c, j, par, turn):
                unit(i, c, False, xt, (0,))
                keys_values(j - 1, par, turn)
                unit(i, c, False, xt, (1,))
                logits(j - 1, par)
                unit(i, c + 1, False, xt, (0,))
                turn_probs(j - 1)
                unit(i, c + 1, False, xt, (1,))
                attend(j - 1)

            ia, ca = U_AQ // 4, U_AQ % 4
            unit(ia, ca, False, xt)
            unit(ia, ca + 1, False, xt)
            sparse_body(ia, ca + 2, 1, 0, 0)
            with pe.Fori(0, PAIRS // 2 - 1) as it:
                sparse_body(it + ia, ca + 4, it * 2 + 2, 1, it)
                sparse_body(it + ia, ca + 6, it * 2 + 3, 0, it + 1)
            keys_values(PAIRS - 1, 1, PAIRS // 2 - 1)
            logits(PAIRS - 1, 1)
            turn_probs(PAIRS - 1)
            attend(PAIRS - 1)

            pe.wait_ge(ob_sb, PAIRS)
            with pe.Fori(0, UPM // 4) as it:
                for n in range(4):
                    unit(it + U_WB // 4, U_WB % 4 + n, False, ob_t)
            pe.wait_ge(mixb_done, UPM + 2)
            with pe.Fori(0, UPM // 4) as it:
                for n in range(4):
                    unit(it + U_MIX // 4, U_MIX % 4 + n, True, mix_t)

            def turn_h(q, turn):
                tb, k4 = q // 4, q % 4
                pe.wait_ge(h_done, 2 * turn + tb + 1)
                n = 8 * turn + q
                if n >= 4:
                    pe.wait_ge(tr_sb, n - 3)
                for k in range(4):
                    ins = transpose(B[q % 4][:, k * P:(k + 1) * P],
                                    h_tok[:, tb * D + (4 * k4 + k) * P:tb * D + (4 * k4 + k + 1) * P])
                ins.then_inc(tr_ps, 1)

            pe.wait_ge(mem_in, 32)
            for j in range(UPM):
                unit(0, U_CV + j, True, mem_b)
                if j >= 4:
                    for q in (2 * (j - 4), 2 * (j - 4) + 1):
                        turn_h(q, 0)

            def cross_logits(m):
                pe.wait_ge(evac_done, U_CQ + 2 * m + 2)
                if m:
                    pe.wait_ge(ce_done, 2 * m)
                for tb in range(TB):
                    for c in range(4):
                        ins = mm(B[0][:, tb * 256:(tb + 1) * 256], qc[m % 2][:, c * 256 + tb * P:c * 256 + (tb + 1) * P],
                                 kc_t[:, (4 * m + c) * 256:(4 * m + c + 1) * 256], start=c == 0, stop=c == 3)
                ins.then_inc(cl_ps, 1)

            def cross_turn(m):
                pe.wait_ge(cp_done, 2 * m + 2)
                if m:
                    pe.wait_ge(ct_sb, m)
                for mb in range(2):
                    for tb in range(TB):
                        ins = transpose(B[1][:, mb * 256 + tb * P:mb * 256 + (tb + 1) * P],
                                        pc[:, tb * 256 + mb * P:tb * 256 + (mb + 1) * P])
                ins.then_inc(ct_ps, 1)

            def cross_out(m):
                pe.wait_ge(ct_sb, m + 1)
                if m:
                    pe.wait_ge(co_sb, m)
                for c in range(4):
                    for mb in range(2):
                        ins = mm(B[2 + c // 2][:, (c % 2) * 256:(c % 2 + 1) * 256],
                                 vc[:, mb * D + m * MEM_DH + c * P:mb * D + m * MEM_DH + (c + 1) * P],
                                 ptc[:, mb * 256:(mb + 1) * 256], start=mb == 0, stop=mb == 1)
                ins.then_inc(co_ps, 1)

            pe.wait_ge(tr_sb, 8)
            for m in range(MEM_HEADS):
                unit(0, U_CQ + 2 * m, False, h_t, (0,))
                if m:
                    cross_logits(m - 1)
                unit(0, U_CQ + 2 * m, False, h_t, (1,))
                if m:
                    cross_turn(m - 1)
                unit(0, U_CQ + 2 * m + 1, False, h_t, (0,))
                if m:
                    cross_out(m - 1)
                unit(0, U_CQ + 2 * m + 1, False, h_t, (1,))
            cross_logits(MEM_HEADS - 1)
            cross_turn(MEM_HEADS - 1)
            cross_out(MEM_HEADS - 1)
            pe.wait_ge(co_sb, MEM_HEADS)
            with pe.Fori(0, UPM // 4) as it:
                for n in range(4):
                    unit(it + U_CO // 4, U_CO % 4 + n, True, oc_t)
            for q in range(8):
                turn_h(q, 1)
            pe.wait_ge(tr_sb, 16)

            def sum_rows(b, Y):
                for e in range(BATCH):
                    pe.wait_ge(diag_done, b * BATCH + e + 1)
                    pe.wait_ge(v_in[e], b * 16 + 16)
                    for c in range(4):
                        ins = mm(Y[c], diag[:, e * P:(e + 1) * P], v_rows[e][:, c * 512:(c + 1) * 512],
                                 start=False, stop=True, skip_group_check=True)
                    ins.then_inc(v_used, 1)

            def residual(tb, Y):
                for c in range(4):
                    mm(Y[c], C[:, K_ALPHA:K_ALPHA + P], h_tok[:, tb * D + c * 512:tb * D + (c + 1) * 512],
                       start=True, stop=True, skip_group_check=True)

            def peer_scores(k):
                unit(0, U_PQ + k, False, h_t, bank=PJ[k % 2])
                pe.wait_ge(evac_done, U_PQ + k + 1)
                if k >= 2:
                    pe.wait_ge(psc_sb, k - 1)
                for tb in range(TB):
                    for h in range(2):
                        ins = mm(PJ[2 + k % 2][:, (tb * 2 + h) * P:(tb * 2 + h + 1) * P],
                                 qp[:, h * 256 + tb * P:h * 256 + (tb + 1) * P],
                                 keys_t[:, (2 * k + h) * P:(2 * k + h + 1) * P], start=True, stop=True)
                ins.then_inc(psc_ps, 1)

            pe.wait_ge(keys_in, 16)
            peer_scores(0)
            residual(0, B)
            peer_scores(1)
            for k in range(1, PEER_HEADS):
                if k + 1 < PEER_HEADS:
                    peer_scores(k + 1)
                sum_rows(2 * k - 2, B)
                sum_rows(2 * k - 1, B)
            with pe.Fori(EARLY, BPB) as b:
                sum_rows(b, B)
            pe.wait_ge(psc_sb, PEER_HEADS)
            residual(1, PJ)
            with pe.Fori(BPB, TB * BPB) as b:
                sum_rows(b, PJ)

        @block.scalar
        def _(act):
            chain = Chain(act, act_chain)
            fn = nc.scalar.activation

            def mark(ins, s, value):
                ins.then_inc(s, 1)
                act.wait_ge(s, value)

            act.wait_ge(rb_ps, 1)
            mark(fn(oh[0:16, 512:896], B[3][0:16, 0:384], ACT.Copy), rb_sb, 1)
            act.wait_ge(lbd_done, 1)
            mark(fn(lbr, lbr, ACT.Exp), lbe_done, 1)

            act.wait_ge(proj_done, U_CKV + 1)
            mark(fn(ckv, PJ[U_CKV], ACT.Copy), evac_done, U_CKV + 1)
            act.wait_ge(proj_done, U_IK + 1)
            mark(fn(ikw, PJ[U_IK], ACT.Copy), evac_done, U_IK + 1)
            for tb in range(TB):
                mark(fn(cn[:, tb * 256:(tb + 1) * 256], ckv[:, tb * 256:(tb + 1) * 256], ACT.Square,
                        accum_out=ss[:, tb:tb + 1]), ss_done, tb + 1)
            act.wait_ge(eps_set, 2)
            act.wait_ge(mv_done, 2)
            chain.link(fn(rs, ss, ACT.Ln, scale=1.0 / 256, bias=eps_rms))
            mark(fn(rs, rs, ACT.Exp, scale=-0.5), rn_done, 1)
            chain.link(fn(g2, mv[:, 1:4:2], ACT.Ln, bias=eps_ln))
            mark(fn(g2, g2, ACT.Exp, scale=-0.5), rn_done, 2)

            def hg_body(p, new, old):
                zero = isinstance(p, int) and p == 0
                u = p * 4 + U_HG
                if new:
                    act.wait_ge(proj_done, u + 1)
                    if not zero:
                        act.wait_ge(f_ready, p)
                    mark(fn(a_sf, PJ[U_HG % 4], ACT.Sigmoid), evac_done, u + 1)
                if old:
                    act.wait_ge(kd_ps, p)
                    mark(fn(a_kd, B[0], ACT.Copy), kd_sb, p)
                if new:
                    act.wait_ge(proj_done, u + 2)
                    if not zero:
                        act.wait_ge(qk_ready, p * 4)
                    mark(fn(a_q, PJ[(U_HG + 1) % 4], ACT.Copy), evac_done, u + 2)
                    act.wait_ge(proj_done, u + 3)
                    if not zero:
                        act.wait_ge(ot_ps, p)
                    mark(fn(a_v, PJ[(U_HG + 2) % 4], ACT.Copy), evac_done, u + 3)
                if old:
                    act.wait_ge(ot_ps, p)
                    act.wait_ge(f_ready, p + 1)
                    mark(fn(a_sq, B[0], ACT.Square), sq_sb, p)
                if zero:
                    act.wait_ge(cn_ps, 1)
                    mark(fn(ckv_t, B[0], ACT.Copy), cn_sb, 1)
                    mark(fn(ik_t, B[1][:, 0:256], ACT.Copy), cn_sb, 2)
                if new:
                    act.wait_ge(proj_done, u + 4)
                    if not zero:
                        act.wait_ge(t2_done, p)
                    mark(fn(a_sg, PJ[(U_HG + 3) % 4], ACT.Sigmoid), gate_rd, p + 1)
                    mark(fn(a_gr, PJ[(U_HG + 3) % 4], ACT.Copy), evac_done, u + 4)
                    act.wait_ge(f_ready, p + 1)
                    mark(fn(a_f, a_f, ACT.Ln), lf_ready, p + 1)
                if old:
                    act.wait_ge(ms_ps, p)
                    chain.link(fn(a_sq, B[1], ACT.Ln, bias=eps_rms))
                    mark(fn(a_sq, a_sq, ACT.Exp, scale=-0.5), rs_sb, p)
                if new:
                    act.wait_ge(g_ready, p + 1)
                    if not zero:
                        act.wait_ge(st_sb, p)
                    for n, (src, scale) in enumerate(((a_gd, 1.0), (a_gd, -1.0), (a_g, 1.0), (a_gl, 1.0))):
                        mark(fn(a_ex[:, n * 512:(n + 1) * 512], src, ACT.Exp, scale=scale), ex_ready, p * 4 + n + 1)

            hg_body(0, True, False)
            with act.Fori(1, PAIRS) as p:
                chain.loop(p - 1, 1)
                hg_body(p, True, True)
                chain.end(PAIRS - 1)

            def keys_out(j):
                act.wait_ge(proj_done, U_CK + j + 1)
                mark(fn(kc_t[:, j * 512:(j + 1) * 512], PJ[(U_CK + j) % 4], ACT.Copy), evac_done, U_CK + j + 1)

            keys_out(0)
            act.wait_ge(kd_ps, PAIRS)
            mark(fn(a_kd, B[0], ACT.Copy), kd_sb, PAIRS)
            keys_out(1)
            keys_out(2)
            act.wait_ge(ot_ps, PAIRS)
            act.wait_ge(oh_done, 2 * PAIRS - 2)
            mark(fn(a_sq, B[0], ACT.Square), sq_sb, PAIRS)
            keys_out(3)
            act.wait_ge(ms_ps, PAIRS)
            chain.link(fn(a_sq, B[1], ACT.Ln, bias=eps_rms))
            mark(fn(a_sq, a_sq, ACT.Exp, scale=-0.5), rs_sb, PAIRS)
            for j in range(4, UPM):
                keys_out(j)

            def relu_out(j):
                act.wait_ge(sidx_ps, j + 1)
                if j >= 2:
                    act.wait_ge(acc_done, j - 1)
                banks = PS[:, 4 + 2 * (j % 2):6 + 2 * (j % 2), 0:384]
                mark(fn(relu[j % 2].rearrange("p (h x) -> p h x", h=2), banks, ACT.Relu, scale=IDX_DIM ** -0.5), relu_sb, j + 1)

            for j in range(UPM):
                act.wait_ge(proj_done, U_IQ + j + 1)
                if j >= 2:
                    act.wait_ge(sidx_ps, j - 1)
                mark(fn(iq[j % 2], PJ[(U_IQ + j) % 4], ACT.Copy), evac_done, U_IQ + j + 1)
                if j:
                    relu_out(j - 1)
            relu_out(UPM - 1)

            with act.Fori(0, UPM // 2) as it:
                for n in range(2):
                    u = it * 4 + U_GA + 2 * n
                    act.wait_ge(proj_done, u + 1)
                    act.wait_ge(mixa_done, it * 2 + n + 1)
                    mark(fn(ga[n], PJ[(U_GA + 2 * n) % 4], ACT.Sigmoid), evac_done, u + 1)
                    act.wait_ge(proj_done, u + 2)
                    mark(fn(yb[n], PJ[(U_GA + 2 * n + 1) % 4], ACT.Copy), evac_done, u + 2)

            def kv_out(j):
                act.wait_ge(kv_ps, j + 1)
                if not (isinstance(j, int) and j == 0):
                    act.wait_ge(lg_ps, j)
                mark(fn(khs, B[0], ACT.Copy), kv_sb, j * 2 + 1)
                if not (isinstance(j, int) and j == 0):
                    act.wait_ge(ob_ps, j)
                mark(fn(vhs, B[1], ACT.Copy), kv_sb, j * 2 + 2)

            def exps(j):
                act.wait_ge(lg_rd, j + 1)
                for g in range(4):
                    h, tb = g // 2, g % 2
                    cols = lg[:, h * 384:h * 384 + 256] if tb == 0 else lg[:, h * 384 + 256:(h + 1) * 384]
                    mark(fn(cols, cols, ACT.Exp, bias=nmax[:, g:g + 1], accum_out=esum[:, g:g + 1]), p_exp, j * 4 + g + 1)

            def probs_out(j):
                act.wait_ge(pt_ps, j + 1)
                if not (isinstance(j, int) and j == 0):
                    act.wait_ge(ob_ps, j)
                mark(fn(pt.rearrange("p (h x) -> p h x", h=2), B23[:, :, 0:384], ACT.Copy), pt_sb, j + 1)

            def attended_out(j):
                act.wait_ge(ob_ps, j + 1)
                mark(fn(ob_t[:, bass.ds(j * 512, 512)], B[0], ACT.Copy), ob_sb, j + 1)

            def q_out(j, bank, par):
                act.wait_ge(proj_done, j * 2 + U_AQ + 1)
                if not (isinstance(j, int) and j < 2):
                    act.wait_ge(lg_ps, j - 1)
                mark(fn(aq[par], bank, ACT.Copy, scale=AT_DH ** -0.5), evac_done, j * 2 + U_AQ + 1)

            def gate_out(j, bank):
                act.wait_ge(proj_done, j * 2 + U_AQ + 2)
                mark(fn(gate_b[:, bass.ds(j * 512, 512)], bank, ACT.Sigmoid), evac_done, j * 2 + U_AQ + 2)

            def sparse_body(j, c, par):
                kv_out(j - 1)
                q_out(j, PJ[c % 4], par)
                exps(j - 1)
                probs_out(j - 1)
                gate_out(j, PJ[(c + 1) % 4])
                attended_out(j - 1)

            q_out(0, PJ[U_AQ % 4], 0)
            gate_out(0, PJ[(U_AQ + 1) % 4])
            sparse_body(1, U_AQ + 2, 1)
            with act.Fori(0, PAIRS // 2 - 1) as it:
                sparse_body(it * 2 + 2, U_AQ + 4, 0)
                sparse_body(it * 2 + 3, U_AQ + 6, 1)
            kv_out(PAIRS - 1)
            exps(PAIRS - 1)
            probs_out(PAIRS - 1)
            attended_out(PAIRS - 1)

            with act.Fori(0, UPM // 4) as it:
                for n in range(4):
                    u = it * 4 + U_WB + n
                    act.wait_ge(proj_done, u + 1)
                    act.wait_ge(mixb_done, it * 4 + n + 1)
                    mark(fn(yb[n % 2], PJ[(U_WB + n) % 4], ACT.Copy), evac_done, u + 1)

            def rows_out(first, z_before):
                with act.Fori(0, UPM // 4) as it:
                    for n in range(4):
                        u = it * 4 + first + n
                        act.wait_ge(proj_done, u + 1)
                        act.wait_ge(z_done, it * 4 + n + z_before + 1)
                        mark(fn(yz[n % 2], PJ[(first + n) % 4], ACT.Copy), evac_done, u + 1)

            rows_out(U_MIX, 0)

            def rstd(turn, tb):
                act.wait_ge(lnv_done, 2 * turn + tb + 1)
                chain.link(fn(rs[:, tb:tb + 1], mv[:, 2 * tb + 1:2 * tb + 2], ACT.Ln, bias=eps_ln))
                mark(fn(rs[:, tb:tb + 1], rs[:, tb:tb + 1], ACT.Exp, scale=-0.5), lnr_done, 2 * turn + tb + 1)

            def turned_out(q, turn):
                tb, k4 = q // 4, q % 4
                n = 8 * turn + q
                act.wait_ge(tr_ps, n + 1)
                dst = h_t.rearrange("p (k t) -> p k t", k=KT)[:, 4 * k4:4 * k4 + 4, tb * P:(tb + 1) * P]
                mark(fn(dst, B[q % 4].rearrange("p (k t) -> p k t", k=4), ACT.Copy), tr_sb, n + 1)

            rstd(0, 0)
            for j in range(UPM):
                act.wait_ge(proj_done, U_CV + j + 1)
                dst = vc.rearrange("p (b n) -> p b n", b=2)[:, :, j * UN:(j + 1) * UN]
                mark(fn(dst, PJ[(U_CV + j) % 4].rearrange("p (b n) -> p b n", b=2), ACT.Copy), evac_done, U_CV + j + 1)
                if j == 0:
                    rstd(0, 1)
                if j >= 4:
                    for q in (2 * (j - 4), 2 * (j - 4) + 1):
                        turned_out(q, 0)

            def cross_exps(m):
                act.wait_ge(cl_rd, m + 1)
                for tb in range(TB):
                    if m:
                        act.wait_ge(ct_ps, m)
                    mark(fn(pc[:, tb * 256:(tb + 1) * 256], B[0][:, tb * 256:(tb + 1) * 256], ACT.Exp, scale=MEM_DH ** -0.5,
                            bias=nmax[:, tb:tb + 1], accum_out=esum[:, tb:tb + 1]), ce_done, 2 * m + tb + 1)

            def cross_turned(m):
                act.wait_ge(ct_ps, m + 1)
                if m:
                    act.wait_ge(co_ps, m)
                mark(fn(ptc, B[1], ACT.Copy), ct_sb, m + 1)

            def cross_attended(m):
                act.wait_ge(co_ps, m + 1)
                mark(fn(oc_t[:, m * 1024:(m + 1) * 1024].rearrange("p (a b) -> p a b", a=2), B23, ACT.Copy), co_sb, m + 1)

            def cq_out(m, n):
                u = U_CQ + 2 * m + n
                act.wait_ge(proj_done, u + 1)
                if m >= 2:
                    act.wait_ge(cl_ps, m - 1)
                mark(fn(qc[m % 2][:, n * 512:(n + 1) * 512], PJ[u % 4], ACT.Copy), evac_done, u + 1)

            for m in range(MEM_HEADS):
                if m:
                    cross_exps(m - 1)
                cq_out(m, 0)
                if m:
                    cross_turned(m - 1)
                    cross_attended(m - 1)
                cq_out(m, 1)
            cross_exps(MEM_HEADS - 1)
            cross_turned(MEM_HEADS - 1)
            cross_attended(MEM_HEADS - 1)

            rows_out(U_CO, UPM)
            for tb in range(TB):
                rstd(1, tb)
            for q in range(8):
                turned_out(q, 1)

            def step(b, first=False):
                act.wait_ge(dot_done, b * BATCH + BATCH)
                if not first:
                    act.wait_ge(v_used, b * BATCH)
                chain.link(fn(hg4, dots, ACT.Gelu))
                for e in range(BATCH):
                    mark(fn(gh4[:, e:e + 1], gates[:, bass.ds(b * BATCH + e, 1)], ACT.Copy, scale=hg4[:, e:e + 1]),
                         gh_done, b * BATCH + e + 1)
                for e in range(BATCH):
                    mark(fn(diag[:, e * P:(e + 1) * P], ident, ACT.Copy, scale=gh4[:, e:e + 1]), diag_done, b * BATCH + e + 1)

            def scores_out(k):
                act.wait_ge(proj_done, U_PQ + k + 1)
                if k:
                    act.wait_ge(psc_ps, k)
                mark(fn(qp, PJ[k % 2], ACT.Copy), evac_done, U_PQ + k + 1)
                act.wait_ge(psc_ps, k + 1)
                if k:
                    act.wait_ge(head_done, k)
                mark(fn(sc, PJ[2 + k % 2], ACT.Copy), psc_sb, k + 1)

            def gates_exp(k):
                act.wait_ge(tops_rd, k + 1)
                mark(fn(e_top, e_top, ACT.Exp), gexp_done, k + 1)

            scores_out(0)
            gates_exp(0)
            scores_out(1)
            for k in range(1, PEER_HEADS):
                gates_exp(k)
                if k + 1 < PEER_HEADS:
                    scores_out(k + 1)
                step(2 * k - 2, k == 1)
                step(2 * k - 1)
            with act.Fori(EARLY, BPB) as b:
                chain.loop(b - EARLY, 1)
                step(b)
                chain.end(BPB - EARLY)
            step(BPB)
            rstd(2, 0)
            with act.Fori(BPB + 1, TB * BPB) as b:
                chain.loop(b - BPB - 1, 1)
                step(b)
                chain.end(BPB - 1)
            rstd(2, 1)

        @block.vector
        def _(dve):
            chain = Chain(dve, dve_chain)
            v = nc.vector
            link = chain.link

            def mark(ins, s, value):
                ins.then_inc(s, 1)
                dve.wait_ge(s, value)

            dve.wait_ge(row_in, 80)
            link(v.tensor_tensor(lbm, lbr[:, 0:16], lbr[:, 16:32], ALU.max))
            link(v.tensor_tensor(lbr[:, 0:16], lbr[:, 0:16], lbm, ALU.subtract))
            mark(v.tensor_tensor(lbr[:, 16:32], lbr[:, 16:32], lbm, ALU.subtract), lbd_done, 1)
            dve.wait_ge(lbe_done, 1)
            link(v.tensor_tensor(lbm, lbr[:, 0:16], lbr[:, 16:32], ALU.add))
            link(v.reciprocal(lbm, lbm))
            link(v.tensor_tensor(lb, lbr[:, 0:16], lbm, ALU.mult))
            link(v.tensor_scalar(omlb, lb, -1.0, 1.0, ALU.mult, ALU.add))
            link(v.memset(a_at, 0.0))
            dve.wait_ge(evac_done, U_IK + 1)
            for tb in range(TB):
                link(v.bn_stats(stats[:, 6 * tb:6 * tb + 6], ikw[:, tb * 256:tb * 256 + P]))
                mark(v.bn_aggr(mv[:, 2 * tb:2 * tb + 2], stats[:, 6 * tb:6 * tb + 6]), mv_done, tb + 1)
            for tb in range(TB):
                link(v.tensor_scalar(iw[:, tb * 16:(tb + 1) * 16], ikw[:, tb * 256 + P:tb * 256 + P + HEADS],
                                     HEADS ** -0.5, None, ALU.mult))
            dve.wait_ge(ss_done, 2)
            dve.wait_ge(rn_done, 2)
            for tb in range(TB):
                cols = ckv[:, tb * 256:(tb + 1) * 256]
                mark(v.scalar_tensor_tensor(cn[:, tb * 256:(tb + 1) * 256], cols, rs[:, tb:tb + 1], row_kv, ALU.mult, ALU.mult),
                     cn_done, tb + 1)
            for tb in range(TB):
                cols = ikw[:, tb * 256:tb * 256 + P]
                link(v.tensor_scalar(cols, cols, mv[:, 2 * tb:2 * tb + 1], g2[:, tb:tb + 1], ALU.subtract, ALU.mult))
                link(v.tensor_tensor(cols, cols, row_ikg, ALU.mult))
                mark(v.tensor_tensor(cols, cols, row_ikb, ALU.add), cn_done, tb + 3)

            def hg_body(p, new, old):
                if new:
                    dve.wait_ge(evac_done, p * 4 + U_HG + 1)
                    for h in range(2):
                        link(v.tensor_scalar(a_f[:, h * 256:(h + 1) * 256], a_sf[:, h * 256:(h + 1) * 256],
                                             omlb[:, bass.ds(p * 2 + h, 1)], lb[:, bass.ds(p * 2 + h, 1)], ALU.mult, ALU.add))
                    mark(v.tensor_scalar(a_k, a_f, -1.0, 1.0, ALU.mult, ALU.add), f_ready, p + 1)
                if old:
                    dve.wait_ge(at_ps, p)
                    dve.sem_inc(at_seen, 1)
                    mask = C[:, K_AMASK:K_AMASK + P].bitcast(U32).unsqueeze(1).to_broadcast([P, 4, P])
                    mark(v.copy_predicated(a_at.rearrange("p (g i) -> p g i", g=4), mask,
                                           B[1].rearrange("p (g i) -> p g i", g=4)), at_sb, p)
                    dve.wait_ge(u_ps, p)
                    st = a_st.rearrange("p (h c n) -> p h c n", h=2, c=3)
                    link(v.tensor_copy(st[:, :, 0, :], B[2][:, 0:256].rearrange("p (h n) -> p h n", h=2)))
                    for c in (1, 2):
                        for h in range(2):
                            last = 1024 + h * 256 + (c + 1) * CHUNK - 1
                            ins = v.scalar_tensor_tensor(st[:, h, c, :], st[:, h, c - 1, :], a_ex[:, last:last + 1],
                                                         update(c, h), ALU.mult, ALU.add)
                            if (c, h) == (2, 1):
                                mark(ins, st_sb, p)
                            else:
                                link(ins)
                    dve.wait_ge(sq_sb, p)
                    mark(v.tensor_tensor(a_t2, B[0], a_gr, ALU.mult), t2_done, p)
                if new:
                    dve.wait_ge(gate_rd, p + 1)
                    dve.wait_ge(evac_done, p * 4 + U_HG + 4)
                    link(v.tensor_tensor(a_gr, a_gr, a_sg, ALU.mult))
                if old:
                    dve.wait_ge(rs_sb, p)
                    for h in range(2):
                        mark(v.scalar_tensor_tensor(oh[:, bass.ds(p * 512 - 512 + h * 256, 256)], a_t2[:, h * 256:(h + 1) * 256],
                                                    hgn[:, bass.ds(p * 2 - 2 + h, 1)], a_sq[:, h * 256:(h + 1) * 256],
                                                    ALU.mult, ALU.mult), oh_done, p * 2 - 1 + h)
                if new:
                    dve.wait_ge(lf_ready, p + 1)
                    link(v.tensor_tensor_scan(a_g, C[:, K_RESET:K_RESET + 512], a_f, 0.0, ALU.mult, ALU.add))
                    g3 = a_g.rearrange("p (c t) -> p c t", t=CHUNK)
                    mid = g3[:, :, CHUNK // 2 - 1:CHUNK // 2].to_broadcast([P, 8, CHUNK])
                    end = g3[:, :, CHUNK - 1:CHUNK].to_broadcast([P, 8, CHUNK])
                    link(v.tensor_tensor(a_gd.rearrange("p (c t) -> p c t", t=CHUNK), g3, mid, ALU.subtract))
                    mark(v.tensor_tensor(a_gl.rearrange("p (c t) -> p c t", t=CHUNK), end, g3, ALU.subtract), g_ready, p + 1)
                    dve.wait_ge(ex_ready, p * 4 + 4)
                    dve.wait_ge(evac_done, p * 4 + U_HG + 2)
                    for n, src in enumerate((a_q, a_k, a_q, a_k)):
                        mark(v.tensor_tensor(a_pr[:, n * 512:(n + 1) * 512], src, a_ex[:, n * 512:(n + 1) * 512], ALU.mult),
                             qk_ready, p * 4 + n + 1)

            dve.wait_ge(const_in, 16)
            hg_body(0, True, False)
            dve.wait_ge(rb_out, 16)
            with dve.Fori(1, PAIRS) as p:
                chain.loop(p - 1, 9)
                hg_body(p, True, True)
                chain.end(PAIRS - 1)
            hg_body(PAIRS, False, True)
            for s in (mixa_done, mixb_done, z_done):
                mark(v.memset(ga[0][:, 0:1], 0.0), s, 1)
                mark(v.memset(ga[0][:, 0:1], 0.0), s, 2)

            dve.wait_ge(cn_ps, 1)
            dve.wait_ge(relu_sb, 1)
            link(v.memset(score, 0.0))
            for j in range(PAIRS):
                dve.wait_ge(relu_sb, j + 1)
                for h in range(2):
                    for tb, lo, hi in ((1, 0, 256), (0, 256, 384)):
                        w = iw[:, tb * 16 + 2 * j + h:tb * 16 + 2 * j + h + 1]
                        ins = v.scalar_tensor_tensor(score[:, lo:hi], relu[j % 2][:, h * 384 + lo:h * 384 + hi], w, score[:, lo:hi],
                                                     ALU.mult, ALU.add)
                        if (h, tb) == (1, 0):
                            mark(ins, acc_done, j + 1)
                        else:
                            link(ins)
            link(v.tensor_tensor(score, score, C[:, K_CAUS:K_CAUS + 384], ALU.add))
            for lo, hi in ((0, 256), (256, 384)):
                with dve.Fori(0, TOPK // 8) as r:
                    chain.loop(r, 2)
                    link(v.max(m8, score[:, lo:hi]))
                    dve.sem_inc(max_seen, 1)
                    link(v.match_replace(score[:, lo:hi], m8, score[:, lo:hi], TAKEN))
                    chain.end(TOPK // 8)
            link(v.tensor_scalar(sel_mask, score, TAKEN / 2, MASKED, ALU.is_gt, ALU.mult))
            mark(v.tensor_tensor(sel_mask, sel_mask, C[:, K_CAUS:K_CAUS + 384], ALU.add), sel_done, 1)

            with dve.Fori(0, UPM // 2) as it:
                for n in range(2):
                    dve.wait_ge(evac_done, it * 4 + U_GA + 2 * n + 2)
                    mark(v.tensor_tensor(mix_t[:, bass.ds(it * 1024 + n * 512, 512)], ga[n], yb[n], ALU.mult),
                         mixa_done, it * 2 + n + 3)

            lg3 = lg.rearrange("p (h x) -> p h x", h=2)
            bias3 = biases.rearrange("p (h x) -> p h x", h=2)
            wide, narrow = slice(0, 256), slice(256, 384)

            def next_biases(j):
                rel = th[:, bass.ds(j * 512, 512)].rearrange("p (h x) -> p h x", h=2)
                for cols, x in ((wide, rel), (narrow, rel[:, :, P:256])):
                    link(v.tensor_tensor(bias3[:, :, cols], x, sel_mask[:, cols].unsqueeze(1).to_broadcast([P, 2, x.shape[2]]), ALU.add))

            def biased(j):
                dve.wait_ge(lg_ps, j + 1)
                if not (isinstance(j, int) and j == 0):
                    dve.wait_ge(pt_ps, j)
                link(v.tensor_tensor(lg3, B23[:, :, 0:384], bias3, ALU.add))
                least = nmax.rearrange("p (h t) -> p h t", h=2)
                link(v.tensor_reduce(least[:, :, 0], lg3[:, :, wide], AX.X, ALU.max, negate=True))
                mark(v.tensor_reduce(least[:, :, 1], lg3[:, :, narrow], AX.X, ALU.max, negate=True), lg_rd, j + 1)

            def normed(j):
                dve.wait_ge(p_exp, j * 4 + 4)
                link(v.reciprocal(rec, esum))
                for n, cols in enumerate((wide, narrow)):
                    r = rec.rearrange("p (h t) -> p h t", h=2)[:, :, n:n + 1].to_broadcast([P, 2, cols.stop - cols.start])
                    mark(v.tensor_tensor(lg3[:, :, cols], lg3[:, :, cols], r, ALU.mult), p_ready, j * 2 + n + 1)

            dve.wait_ge(th_in, 16)
            next_biases(0)
            biased(0)
            normed(0)
            next_biases(1)
            with dve.Fori(1, PAIRS - 1) as j:
                chain.loop(j - 1, 5)
                biased(j)
                normed(j)
                next_biases(j + 1)
                chain.end(PAIRS - 2)
            biased(PAIRS - 1)
            normed(PAIRS - 1)

            with dve.Fori(0, UPM // 2) as it:
                chain.loop(it, 2)
                for n in range(2):
                    dve.wait_ge(evac_done, it * 2 + n + U_WB + 1)
                    cols = mix_t[:, bass.ds(it * 1024 + n * 512, 512)]
                    link(v.tensor_tensor(yb[n], gate_b[:, bass.ds(it * 1024 + n * 512, 512)], yb[n], ALU.mult))
                    mark(v.tensor_tensor(cols, cols, yb[n], ALU.add), mixb_done, it * 2 + n + 3)
                chain.end(UPM // 2)

            def add_residual(first, before):
                with dve.Fori(0, UPM // 2) as it:
                    chain.loop(it, 6)
                    for n in range(2):
                        dve.wait_ge(evac_done, it * 2 + n + first + 1)
                        for tb in range(TB):
                            cols = h_tok[:, bass.ds(it * 512 + n * 256 + tb * D, 256)]
                            link(v.scalar_tensor_tensor(cols, cols, ALPHA, yz[n][:, tb * 256:(tb + 1) * 256], ALU.mult, ALU.add))
                            ins = v.bn_stats(stats[:, bass.ds(it * 12 + n * 6 + tb * 48, 6)], cols)
                            if tb:
                                mark(ins, z_done, it * 2 + n + before + 3)
                            else:
                                link(ins)
                    chain.end(UPM // 2)

            def norm(turn):
                for tb in range(TB):
                    mark(v.bn_aggr(mv[:, 2 * tb:2 * tb + 2], stats[:, tb * 48:(tb + 1) * 48]), lnv_done, 2 * turn + tb + 1)
                dve.wait_ge(ln_in, 32 * turn + 32)
                for tb in range(TB):
                    dve.wait_ge(lnr_done, 2 * turn + tb + 1)
                    rows = h_tok[:, tb * D:(tb + 1) * D]
                    link(v.tensor_scalar(rows, rows, mv[:, 2 * tb:2 * tb + 1], rs[:, tb:tb + 1], ALU.subtract, ALU.mult))
                    link(v.tensor_tensor(rows, rows, ln_g, ALU.mult))
                    mark(v.tensor_tensor(rows, rows, ln_b, ALU.add), h_done, 2 * turn + tb + 1)

            dve.wait_ge(xtok_in, 16)
            add_residual(U_MIX, 0)
            norm(0)

            for m in range(MEM_HEADS):
                dve.wait_ge(cl_ps, m + 1)
                link(v.reduce_max(nmax2[:, 0:2], B[0].rearrange("p (b n) -> p b n", b=2), AX.X))
                mark(v.tensor_scalar(nmax[:, 0:2], nmax2[:, 0:2], -MEM_DH ** -0.5, None, ALU.mult), cl_rd, m + 1)
                dve.wait_ge(ce_done, 2 * m + 2)
                link(v.reciprocal(rec[:, 0:2], esum[:, 0:2]))
                for tb in range(TB):
                    cols = pc[:, tb * 256:(tb + 1) * 256]
                    mark(v.tensor_scalar(cols, cols, rec[:, tb:tb + 1], None, ALU.mult), cp_done, 2 * m + tb + 1)

            add_residual(U_CO, UPM)
            norm(1)

            def top16(vals, idx, src, rest):
                link(v.max(vals[:, 0:8], src))
                link(v.max_index(idx[:, 0:8], vals[:, 0:8], src))
                link(v.match_replace(rest, vals[:, 0:8], src, TAKEN))
                link(v.max(vals[:, 8:16], rest))
                link(v.max_index(idx[:, 8:16], vals[:, 8:16], rest))

            def head(k):
                dve.wait_ge(psc_sb, k + 1)
                for g in range(4):
                    top16(v16[:, g * PK:(g + 1) * PK], i16[:, g * PK:(g + 1) * PK], sc[:, g * P:(g + 1) * P],
                          sc2[:, g * P:(g + 1) * P])
                link(v.tensor_copy(i16f, i16))
                for tb in range(TB):
                    cols = cand[:, tb * 256:(tb + 1) * 256]
                    rows = v16[:, 2 * tb * PK:(2 * tb + 1) * PK].unsqueeze(2).to_broadcast([P, PK, PK])
                    other = v16[:, (2 * tb + 1) * PK:(2 * tb + 2) * PK].unsqueeze(1).to_broadcast([P, PK, PK])
                    link(v.tensor_tensor(cols.rearrange("p (a b) -> p a b", a=PK), rows, other, ALU.add))
                    top16(top_s[:, tb * PK:(tb + 1) * PK], pos[:, tb * PK:(tb + 1) * PK], cols, cols)
                link(v.tensor_scalar(posh[:, 0:32], pos, 4, None, ALU.logical_shift_right))
                link(v.tensor_scalar(posh[:, 32:64], pos, PK - 1, None, ALU.bitwise_and))
                link(v.tensor_copy(poshf, posh))
                halves = i16f.rearrange("p (t h a) -> p t h a", t=TB, h=2)
                for h in range(2):
                    at3 = poshf[:, h * 32:(h + 1) * 32].unsqueeze(2).to_broadcast([P, 32, PK])
                    count = C[:, K_IOTA:K_IOTA + PK].unsqueeze(1).to_broadcast([P, 32, PK])
                    link(v.tensor_tensor(eq.rearrange("p (r a) -> p r a", a=PK), at3, count, ALU.is_equal))
                    eq4 = eq.rearrange("p (t r a) -> p t r a", t=TB, a=PK)
                    link(v.tensor_tensor(eq4, eq4, halves[:, :, h, :].unsqueeze(2).to_broadcast([P, TB, PK, PK]), ALU.mult))
                    link(v.reduce_sum(idxh[:, h * 32:(h + 1) * 32], eq.rearrange("p (r a) -> p r a", a=PK), AX.X))
                mine = experts.rearrange("p (t e) -> p t e", t=TB)[:, :, k * PK:(k + 1) * PK]
                two = idxh.rearrange("p (h t r) -> p h t r", h=2, t=TB)
                link(v.scalar_tensor_tensor(mine, two[:, 0], float(NKEYS), two[:, 1], ALU.mult, ALU.add))
                best = top_s.rearrange("p (t r) -> p t r", t=TB)
                e3 = e_top.rearrange("p (t r) -> p t r", t=TB)
                mark(v.tensor_tensor(e3, best, best[:, :, 0:1].to_broadcast([P, TB, PK]), ALU.subtract), tops_rd, k + 1)
                dve.wait_ge(gexp_done, k + 1)
                link(v.reduce_sum(g2, e3, AX.X))
                link(v.reciprocal(g2, g2))
                mark(v.tensor_tensor(gates.rearrange("p (t e) -> p t e", t=TB)[:, :, k * PK:(k + 1) * PK], e3,
                                     g2.unsqueeze(2).to_broadcast([P, TB, PK]), ALU.mult), head_done, k + 1)

            def set_idx(b, par, fresh=False):
                if not fresh:
                    for e in range(BATCH):
                        dve.wait_ge(v_in[e], b * 16 - 16)
                        dve.wait_ge(u_in[e], b * 16 - 16)
                mark(v.tensor_copy(idx_fix[:, par * BATCH:(par + 1) * BATCH], experts[:, bass.ds(b * BATCH, BATCH)]), idx_set, b + 1)

            def products(b, tb, fresh=False):
                if not fresh:
                    dve.wait_ge(gh_done, b * BATCH)
                for e in range(BATCH):
                    dve.wait_ge(u_in[e], b * 16 + 16)
                    mark(v.tensor_tensor_reduce(u_rows[e], u_rows[e], h_tok[:, tb * D:(tb + 1) * D], 1.0, 0.0, ALU.mult, ALU.add,
                                                dots[:, e:e + 1]), dot_done, b * BATCH + e + 1)

            def last_norm(tb, Y):
                dve.wait_ge(v_used, (tb + 1) * BPB * BATCH)
                for c in range(4):
                    link(v.bn_stats(stats[:, c * 6:(c + 1) * 6], Y[c]))
                mark(v.bn_aggr(mv[:, 2 * tb:2 * tb + 2], stats[:, 0:24]), lnv_done, 5 + tb)
                dve.wait_ge(lnr_done, 5 + tb)
                if tb:
                    dve.wait_ge(out_done, 16)
                for c in range(4):
                    link(v.tensor_scalar(fin_x[:, c * 512:(c + 1) * 512], Y[c], mv[:, 2 * tb:2 * tb + 1], rs[:, tb:tb + 1],
                                         ALU.subtract, ALU.mult))
                dve.wait_ge(fin_in, 32)
                link(v.tensor_tensor(fin_x, fin_x, fin_g, ALU.mult))
                mark(v.tensor_tensor(fin_x, fin_x, fin_b, ALU.add), fin_done, tb + 1)

            head(0)
            set_idx(0, 0, True)
            for k in range(1, PEER_HEADS):
                head(k)
                for b in (2 * k - 2, 2 * k - 1):
                    set_idx(b + 1, (b + 1) % 2, b == 0)
                    products(b, 0, b == 0)
            with dve.Fori(EARLY // 2, BPB // 2) as i:
                for n in range(2):
                    set_idx(i * 2 + n + 1, 1 - n)
                    products(i * 2 + n, 0)
            set_idx(BPB + 1, 1)
            products(BPB, 1)
            last_norm(0, B)
            with dve.Fori(BPB // 2, TB * BPB // 2 - 1) as i:
                for n in range(2):
                    set_idx(i * 2 + n + 2, n)
                    products(i * 2 + n + 1, 1)
            products(TB * BPB - 1, 1)
            last_norm(1, PJ)


def columns(a):
    return a.reshape(a.shape[0], KT, P).transpose(2, 1, 0).reshape(P, KT * a.shape[0])


def as_units(w):
    n = w.shape[1] // UN
    return w.reshape(KT, P, n, UN).transpose(2, 1, 0, 3).reshape(n, P, KT * UN)


def kernel(**inputs):
    import concourse.bacc as bacc
    from concourse.bass_utils import run_bass_kernel_spmd

    a = {k: np.ascontiguousarray(v) for k, v in inputs.items()}
    x, mem = a["x"][0], a["mem"][0]
    w_in = a["w_in"][0]

    def cut(at, j):
        return as_units(w_in[:, at + UN * j:at + UN * (j + 1)])[0]

    one = [as_units(a[n][0]) for n in ("w_branch_a", "w_branch_b", "w_mix_out", "w_ck", "w_cv", "w_cq", "w_co", "w_pq")]
    w_a, w_b, w_mix, w_ck, w_cv, w_cq, w_co, w_pq = one
    order = [cut(C_CKV, 0), cut(C_IK, 0)]
    for j in range(UPM):
        order += [cut(C_HF, j), cut(C_HQ, j), cut(C_HI, j), cut(C_HG, j)]
    order += list(w_ck)
    order += [cut(C_IQ, j) for j in range(UPM)]
    for j in range(UPM):
        order += [cut(C_GA, j), w_a[j]]
    for j in range(UPM):
        order += [cut(C_AQ, j), cut(C_GB, j)]
    order += list(w_b) + list(w_mix) + list(w_cv) + list(w_cq) + list(w_co) + list(w_pq)
    assert len(order) == UNITS

    def low_rank(w):
        return w.reshape(PAIRS, 2, 2, P, P).transpose(0, 3, 2, 1, 4).reshape(PAIRS, P, 512)

    arrays = {
        "x_tok": x.reshape(TB, P, D).transpose(1, 0, 2).reshape(P, TB * D),
        "x_cols": columns(x),
        "mem_cols": columns(mem),
        "units": np.stack(order),
        "const": constants(),
        "hits": bucket_hits(),
        "rel_bias": a["rel_bias"],
        "lb_logits": a["lb_logits"].reshape(2, HEADS, P).transpose(2, 0, 1).reshape(P, 2 * HEADS),
        "hg_norm": a["hg_norm_g"][0].reshape(HEADS, P).T,
        "kv_g": a["kv_norm_g"][0],
        "ik_g": a["ik_norm_g"][0],
        "ik_b": a["ik_norm_b"][0],
        "w_ukv": np.concatenate([low_rank(a["w_uk"][0]), low_rank(a["w_uv"][0])], axis=2),
        "keys_cols": a["peer_keys"][0].reshape(2 * PEER_HEADS, NKEYS, P).transpose(2, 0, 1).reshape(P, 2 * PEER_HEADS * NKEYS),
        "ln_rows": np.concatenate([a[n] for n in ("ln1_g", "ln1_b", "ln2_g", "ln2_b", "ln3_g", "ln3_b")]),
        "peer_u": a["peer_u"][0],
        "peer_v": a["peer_v"][0],
    }
    arrays = {k: np.ascontiguousarray(v) for k, v in arrays.items()}
    nc = bacc.Bacc("TRN2", target_bir_lowering=False, num_devices=1)
    args = [nc.dram_tensor(n, v.shape, mybir.dt.from_np(v.dtype), kind="ExternalInput").ap() for n, v in arrays.items()]
    rb_scratch = nc.dram_tensor("rb_scratch", (HEADS, P, 384), F32, kind="Internal").ap()
    out = nc.dram_tensor("out", (TB, P, D), F32, kind="ExternalOutput").ap()
    trunk_layer(nc, *args, rb_scratch, out)
    r = run_bass_kernel_spmd(nc, [arrays], core_ids=[0])
    return r.results[0]["out"].reshape(1, SEQ, D)
```

```python
import math
from contextlib import ExitStack

import numpy as np

import concourse.bass as bass
from concourse import mybir

F32 = mybir.dt.float32
U32 = mybir.dt.uint32
ALU = mybir.AluOpType
ACT = mybir.ActivationFunctionType
AX = mybir.AxisListType

P = 128
D = 2048
SEQ = 256
TB = SEQ // P
KT = D // P
UN = 256
UPM = D // UN
DEPTH = 1
ALPHA = (2.0 * DEPTH) ** 0.25
LN_EPS = 1e-5
RMS_EPS = 1e-6
HEADS = 16
PAIRS = HEADS // 2
CHUNK = 64
NCH = SEQ // CHUNK
AT_DH = 128
IDX_DIM = 128
TOPK = min(256, SEQ // 4)
REL_BUCKETS = 32
REL_MAX_DIST = 128
MEM_HEADS = 4
MEM_DH = D // MEM_HEADS
PEER_HEADS = 8
NKEYS = 128
PK = 16
NE = PEER_HEADS * PK
BATCH = 4
BPB = NE // BATCH
PIECES = 4
EARLY = 2 * PEER_HEADS - 1
MASKED = -1e30
TAKEN = -3e38

C_HQ, C_HF, C_HI, C_HG, C_AQ = 0, D, 2 * D, 3 * D, 4 * D
C_CKV = 5 * D
C_IQ = C_CKV + 256
C_IK = C_IQ + D
IK_COLS = IDX_DIM + HEADS
C_GA = C_IK + IK_COLS
C_GB = C_GA + D

U_CKV, U_IK = 0, 1
U_HG = 2
U_CK = U_HG + 4 * PAIRS
U_IQ = U_CK + UPM
U_GA = U_IQ + UPM
U_AQ = U_GA + 2 * UPM
U_WB = U_AQ + 2 * UPM
U_MIX = U_WB + UPM
U_CV = U_MIX + UPM
U_CQ = U_CV + UPM
U_CO = U_CQ + UPM
U_PQ = U_CO + UPM
UNITS = U_PQ + UPM

K_ID, K_MEAN, K_AMASK, K_RESET, K_CAUS, K_IOTA = 0, 128, 256, 384, 896, 1280
K_ALPHA = 1296
K_END = 1424


def constants():
    c = np.zeros((P, K_END), np.float32)
    i = np.arange(P)
    c[:, K_ID:K_ID + P] = np.eye(P)
    c[:, K_MEAN:K_MEAN + P] = 1.0 / P
    c[:, K_AMASK:K_AMASK + P] = (i[:, None] <= i[None, :]) & (i[:, None] // CHUNK == i[None, :] // CHUNK)
    c[:, K_RESET:K_RESET + 512] = (np.arange(512) % CHUNK != 0)[None, :]
    c[:, K_CAUS:K_CAUS + 256] = np.where(np.arange(256)[None, :] <= P + i[:, None], 0.0, MASKED)
    c[:, K_CAUS + 256:K_CAUS + 384] = np.where(i[None, :] <= i[:, None], 0.0, MASKED)
    c[:, K_IOTA:K_IOTA + PK] = np.arange(PK)[None, :]
    c[:, K_ALPHA:K_ALPHA + P] = np.eye(P) * ALPHA
    return c


def bucket_hits():
    dist = np.maximum(255 - np.arange(384), 0)
    exact = REL_BUCKETS // 2
    large = exact + (np.log(np.maximum(dist, 1) / exact) / math.log(REL_MAX_DIST / exact) * (REL_BUCKETS - exact)).astype(np.int64)
    bucket = np.where(dist < exact, dist, np.minimum(large, REL_BUCKETS - 1))
    return (bucket[None, :] == np.arange(REL_BUCKETS)[:, None]).astype(np.float32)


class Chain:

    def __init__(self, eng, sem):
        self.eng, self.sem, self.base, self.k = eng, sem, 0, 0

    def link(self, ins):
        ins.then_inc(self.sem, 1)
        self.k += 1
        self.eng.wait_ge(self.sem, self.base + self.k)

    def loop(self, i, per):
        self.outer = self.base + self.k
        self.base, self.k, self.per = self.outer + i * per, 0, per

    def end(self, times):
        assert self.k == self.per, (self.k, self.per)
        self.base, self.k = self.outer + times * self.per, 0


def trunk_layer(nc, x_tok, x_cols, mem_cols, units, const, hits, rel_bias, lb_logits, hg_norm, ln2_cols, kv_g, ik_g, ik_b,
                w_ukv, keys_cols, ln_rows, peer_u, peer_v, rb_scratch, out):
    with ExitStack() as ctx:
        def sem(name):
            return ctx.enter_context(nc.semaphore(name))

        arena = ctx.enter_context(nc.sbuf_tensor("arena", [P, 52900], F32))
        top = [0]

        def take(n):
            top[0] += n
            assert top[0] <= 52900
            return arena[:, top[0] - n:top[0]]

        def inside(region, at, n):
            return region[:, at:at + n]

        w_ring = take(4 * 4096)
        W = [inside(w_ring, 4096 * s, 4096) for s in range(4)]
        R_X, R_O, R_M, R_B, R_K = (take(4096) for _ in range(5))
        R_S = take(13312)
        C = take(K_END)
        ckv_t = take(512)
        ik_t = take(256)
        iw = take(32)
        small = take(192)
        stats = take(96)
        idx_fix = take(2 * BATCH).bitcast(U32)
        xt = R_X
        h_tok = R_X
        oh = R_O
        gate_b = R_O
        h_t = R_O
        mem_a = R_M
        mix_t = R_M
        oc_t = R_M
        ckv = inside(R_B, 0, 512)
        ikw = inside(R_B, 512, 512)
        cn = inside(R_B, 1024, 512)
        row_kv = inside(R_B, 1536, 256)
        row_ikg = inside(R_B, 1792, 128)
        row_ikb = inside(R_B, 1920, 128)
        iq = [inside(R_B, 2048 + 512 * n, 512) for n in range(2)]
        relu = [inside(R_B, 768 * n, 768) for n in range(2)]
        score = inside(R_B, 3072, 384)
        ob_t = R_B
        mem_b = R_B
        kc_t = R_K
        at = [0]

        def part(n):
            at[0] += n
            assert at[0] <= 13312
            return inside(R_S, at[0] - n, n)

        a_sf, a_q, a_v, a_sg, a_gr, a_f, a_k, a_g, a_gd, a_gl, a_t2, a_sq = (part(512) for _ in range(12))
        a_ex, a_pr = part(2048), part(2048)
        a_kd, a_at = part(512), part(512)
        a_st = part(768)
        at[0] = 0
        th = part(HEADS * 256)
        wukv = [part(1024) for _ in range(2)]
        aq = [part(512) for _ in range(2)]
        khs, vhs = part(512), part(512)
        lg, pt = part(768), part(768)
        sel_mask = part(384)
        biases = part(768)
        ga = [part(512) for _ in range(2)]
        yb = [part(512) for _ in range(2)]
        at[0] = 0
        vc = part(4096)
        ln_g, ln_b = part(D), part(D)
        qc = [part(1024) for _ in range(2)]
        pc, ptc = part(512), part(512)
        yz = [part(512) for _ in range(2)]
        at[0] = 8192
        qp = part(512)
        sc, sc2 = part(512), part(512)
        cand = part(512)
        eq = part(512)
        gates = part(TB * NE)
        experts = part(TB * NE).bitcast(U32)
        v16 = part(64)
        i16 = part(64).bitcast(U32)
        i16f = part(64)
        top_s, e_top = part(PK), part(PK)
        pos = part(PK).bitcast(U32)
        posh = part(2 * PK).bitcast(U32)
        poshf = part(2 * PK)
        idxh = part(2 * PK)
        dots, hg4, gh4 = part(BATCH), part(BATCH), part(BATCH)
        diag = part(BATCH * P)
        keys_t = inside(R_K, 0, 2048)
        u_rows = [inside(R_M, 0, D), inside(R_M, D, D), inside(R_B, 0, D), inside(R_B, D, D)]
        v_rows = [inside(R_S, D * n, D) for n in (2, 3, 0, 1)]
        pq_side = [R_B, inside(R_S, 0, 4096)]
        assert at[0] <= 12288
        fin_g = inside(R_K, D, D)
        fin_b = [inside(C, K_MEAN, 512), inside(C, K_MEAN + 512, 512), inside(R_S, 12288, 512), inside(R_S, 12800, 512)]
        fin_x = inside(w_ring, 2 * D, D)

        ident, mean_m = inside(C, K_ID, P), inside(C, K_MEAN, P)
        lbr = inside(small, 0, 32)
        lb = inside(small, 32, 16)
        omlb = inside(small, 48, 16)
        hgn = inside(small, 64, 16)
        lbm = inside(small, 80, 16)
        ss, rs = inside(small, 96, 2), inside(small, 98, 2)
        mv = inside(small, 100, 4)
        m8 = inside(small, 104, 8)
        nmax, esum, rec = inside(small, 112, 4), inside(small, 116, 4), inside(small, 120, 4)
        eps_ln, eps_rms = inside(small, 124, 1), inside(small, 125, 1)
        g2 = inside(small, 126, 2)
        nmax2 = inside(small, 128, 4)
        warm = inside(small, 132, 1)
        ln2_g, ln2_b = inside(small, 136, KT), inside(small, 152, KT)

        PS = ctx.enter_context(nc.psum_tensor("PS", [P, 8, 512], F32))
        PJ = [PS[:, b, :] for b in range(4)]
        B = [PS[:, 4 + b, :] for b in range(4)]
        B01, B23 = PS[:, 4:6, :], PS[:, 6:8, :]

        def update(c, h):
            return B[3][:, h * P:(h + 1) * P] if c == 1 else B[2][:, (c + h) * P:(c + h + 1) * P]

        w_landed = [sem(f"w_landed{s}") for s in range(4)]
        proj_done = sem("proj_done")
        evac_done = sem("evac_done")
        act_chain, dve_chain = sem("act_chain"), sem("dve_chain")
        const_in, mem_in, row_in, rb_in, rb_out = (sem(n) for n in ("const_in", "mem_in", "row_in", "rb_in", "rb_out"))
        x_in = [sem(f"x_in{n}") for n in range(PIECES)]
        w0_in = [sem(f"w0_in{n}") for n in range(PIECES - 1)]
        th_in, xtok_in = sem("th_in"), sem("xtok_in")
        ukv_in = [sem(f"ukv_in{n}") for n in range(2)]
        keys_in, ln_in, fin_in, out_done = sem("keys_in"), sem("ln_in"), sem("fin_in"), sem("out_done")
        f_ready, lf_ready, g_ready, ex_ready, qk_ready = (sem(n) for n in ("f_ready", "lf_ready", "g_ready", "ex_ready", "qk_ready"))
        kd_ps, kd_sb, at_ps, at_sb, u_ps, st_sb, ot_ps, sq_sb, ms_ps, rs_sb, t2_done, gate_rd, oh_done = (
            sem(n) for n in ("kd_ps", "kd_sb", "at_ps", "at_sb", "u_ps", "st_sb", "ot_ps", "sq_sb", "ms_ps", "rs_sb",
                             "t2_done", "gate_rd", "oh_done"))
        ss_done, mv_done, rn_done, cn_done, cn_ps, cn_sb, eps_set, rb_ps = (
            sem(n) for n in ("ss_done", "mv_done", "rn_done", "cn_done", "cn_ps", "cn_sb", "eps_set", "rb_ps"))
        rb_sb = sem("rb_sb")
        lbe_done, lbd_done = sem("lbe_done"), sem("lbd_done")
        sidx_ps, relu_sb, acc_done = sem("sidx_ps"), sem("relu_sb"), sem("acc_done")
        sel_done = sem("sel_done")
        mixa_done, mixb_done = sem("mixa_done"), sem("mixb_done")
        kv_ps, kv_sb, lg_ps, lg_rd, p_exp, p_ready, pt_ps, pt_sb, ob_ps, ob_sb = (
            sem(n) for n in ("kv_ps", "kv_sb", "lg_ps", "lg_rd", "p_exp", "p_ready", "pt_ps", "pt_sb", "ob_ps", "ob_sb"))
        z_done, lnv_done, lnr_done, h_done, tr_ps, tr_sb = (
            sem(n) for n in ("z_done", "lnv_done", "lnr_done", "h_done", "tr_ps", "tr_sb"))
        last0_ps, last0_sb, bank_done = sem("last0_ps"), sem("last0_sb"), sem("bank_done")
        ln2c_in, unit_var, h_scaled, tv_sb = sem("ln2c_in"), sem("unit_var"), sem("h_scaled"), sem("tv_sb")
        h_final = [sem(f"h_final{n}") for n in range(TB)]
        side_in = [sem(f"side_in{n}") for n in range(2)]
        cl_ps, cl_rd, ce_done, cp_done, ct_ps, ct_sb, co_ps, co_sb = (
            sem(n) for n in ("cl_ps", "cl_rd", "ce_done", "cp_done", "ct_ps", "ct_sb", "co_ps", "co_sb"))
        psc_ps, psc_sb, tops_rd, gexp_done, head_done = (
            sem(n) for n in ("psc_ps", "psc_sb", "tops_rd", "gexp_done", "head_done"))
        q0_ps, q0_sb = sem("q0_ps"), sem("q0_sb")
        idx_set = sem("idx_set")
        u_in = [sem(f"u_in{n}") for n in range(BATCH)]
        v_in = [sem(f"v_in{n}") for n in range(BATCH)]
        dot_done, gh_done, diag_done, v_used = sem("dot_done"), sem("gh_done"), sem("diag_done"), sem("v_used")
        fin_done = sem("fin_done")
        u_slot_free, v_slot_free, idx_seen, at_seen, max_seen = (
            sem(n) for n in ("u_slot_free", "v_slot_free", "idx_seen", "at_seen", "max_seen"))

        block = ctx.enter_context(nc.Block())

        @block.sync
        def _(sp):
            for n in range(PIECES):
                cols = slice(n * 4096 // PIECES, (n + 1) * 4096 // PIECES)
                sp.dma_start(xt[:, cols], x_cols[:, cols]).then_inc(x_in[n], 16)
                sp.dma_start(W[0][:, cols], units[0][:, cols]).then_inc(w_landed[0] if n == PIECES - 1 else w0_in[n], 16)
            for u in range(1, 4):
                sp.dma_start(W[u], units[u]).then_inc(w_landed[u], 16)
                if u == 1:
                    sp.dma_start(C, const).then_inc(const_in, 16)
            whole = (U_PQ - 4) // 4
            with sp.Fori(0, whole) as i:
                for s in range(4):
                    sp.wait_ge(proj_done, i * 4 + s + 1)
                    sp.dma_start(W[s], units[bass.ds(i * 4 + s + 4, 1)].rearrange("a p n -> (a p) n")).then_inc(w_landed[s], 16)
            for u in range(4 + 4 * whole, U_PQ):
                sp.wait_ge(proj_done, u - 3)
                sp.dma_start(W[u % 4], units[u]).then_inc(w_landed[u % 4], 16)
            for n in range(2):
                sp.dma_start(pq_side[n], units[U_PQ + n]).then_inc(side_in[n], 16)
            for n, last in ((4, U_PQ - 4), (5, U_PQ - 3), (2, U_PQ - 2), (3, U_PQ - 1), (6, U_PQ + 2), (7, U_PQ + 3)):
                u = U_PQ + n
                sp.wait_ge(proj_done, last + 1)
                sp.dma_start(W[u % 4], units[u]).then_inc(w_landed[u % 4], 16)
            for tb in range(TB):
                for c in range(4):
                    sp.wait_ge(fin_done, 4 * tb + c + 1)
                    sp.dma_start(out[tb][:, c * 512:(c + 1) * 512], fin_x[:, c * 512:(c + 1) * 512]).then_inc(out_done, 16)
            sp.wait_ge(out_done, 16 * 4 * TB)

        @block.gpsimd
        def _(pool):
            nc.gpsimd.memset(eps_ln, LN_EPS).then_inc(eps_set, 1)
            nc.gpsimd.memset(eps_rms, RMS_EPS).then_inc(eps_set, 1)
            pool.dma_start(lbr, lb_logits).then_inc(row_in, 16)
            pool.dma_start(hgn, hg_norm).then_inc(row_in, 16)
            pool.dma_start(inside(small, 136, 2 * KT), ln2_cols).then_inc(ln2c_in, 16)
            pool.dma_start(row_kv, kv_g.partition_broadcast(P)).then_inc(row_in, 16)
            pool.dma_start(row_ikg, ik_g.partition_broadcast(P)).then_inc(row_in, 16)
            pool.dma_start(row_ikb, ik_b.partition_broadcast(P)).then_inc(row_in, 16)
            pool.dma_start(oh[0:32, 0:384], hits).then_inc(rb_in, 16)
            pool.dma_start(oh[0:32, 384:400], rel_bias).then_inc(rb_in, 16)
            pool.wait_ge(rb_sb, 1)
            pool.dma_start(rb_scratch, oh[0:16, 512:896].unsqueeze(1).to_broadcast([16, P, 384])).then_inc(rb_out, 16)
            pool.dma_start(mem_a, mem_cols).then_inc(mem_in, 16)
            pool.wait_ge(rb_out, 16)
            pool.wait_ge(oh_done, 2 * PAIRS)
            pool.dma_start(th.rearrange("p (h x) -> p h x", h=HEADS),
                           bass.AP(rb_scratch.tensor, 127, [[383, P], [P * 384, HEADS], [1, 256]])).then_inc(th_in, 16)
            for j in range(PAIRS):
                if j >= 2:
                    pool.wait_ge(kv_ps, j - 1)
                pool.dma_start(wukv[j % 2], w_ukv[j]).then_inc(ukv_in[j % 2], 16)
            pool.wait_ge(proj_done, U_WB)
            pool.dma_start(h_tok, x_tok).then_inc(xtok_in, 16)
            pool.wait_ge(proj_done, U_MIX)
            pool.dma_start(mem_b, mem_cols).then_inc(mem_in, 16)
            for n in range(2):
                if n:
                    pool.wait_ge(h_done, 2)
                else:
                    pool.wait_ge(mixb_done, UPM + 2)
                pool.dma_start(ln_g, ln_rows[2 * n].partition_broadcast(P)).then_inc(ln_in, 16)
                pool.dma_start(ln_b, ln_rows[2 * n + 1].partition_broadcast(P)).then_inc(ln_in, 16)
            pool.wait_ge(cl_ps, MEM_HEADS)
            pool.dma_start(keys_t, keys_cols).then_inc(keys_in, 16)
            pool.dma_start(fin_g, ln_rows[4].partition_broadcast(P)).then_inc(fin_in, 16)
            pool.wait_ge(sel_done, 1)
            pool.wait_ge(ms_ps, PAIRS)
            pool.wait_ge(mixb_done, UPM + 2)
            for c in range(4):
                pool.dma_start(fin_b[c], ln_rows[5][c * 512:(c + 1) * 512].partition_broadcast(P)).then_inc(fin_in, 16)
            def gather(b, par, fresh=False):
                pool.wait_ge(idx_set, b + 1)
                pool.sem_inc(idx_seen, 1)
                for e in range(BATCH):
                    if not fresh:
                        pool.wait_ge(dot_done, BATCH * (b - 1) + e + 1)
                        pool.sem_inc(u_slot_free, 1)
                    elif e == 0:
                        pool.wait_ge(proj_done, U_PQ)
                    elif e == 2:
                        pool.wait_ge(proj_done, U_PQ + 1)
                    nc.gpsimd.indirect_dma_start(
                        out=u_rows[e], out_offset=None, in_=peer_u,
                        in_offset=bass.IndirectOffsetOnAxis(ap=idx_fix[:, par * BATCH + e:par * BATCH + e + 1], axis=0),
                    ).then_inc(u_in[e], 16)
                if fresh:
                    rows = h_tok[:, D:2 * D]
                    pool.wait_ge(ln_in, 64)
                    pool.wait_ge(tr_ps, 16)
                    nc.gpsimd.tensor_tensor(rows, rows, ln_g, ALU.mult).then_inc(h_scaled, 1)
                    pool.wait_ge(h_scaled, 1)
                    nc.gpsimd.tensor_tensor(rows, rows, ln_b, ALU.add).then_inc(h_final[1], 1)
                for e in range(BATCH):
                    if not fresh:
                        pool.wait_ge(v_used, BATCH * (b - 1) + e + 1)
                        pool.sem_inc(v_slot_free, 1)
                    elif e == 0:
                        for tb in range(TB):
                            pool.wait_ge(h_final[tb], 1)
                    elif e == 2:
                        pool.wait_ge(proj_done, U_PQ + 2)
                    nc.gpsimd.indirect_dma_start(
                        out=v_rows[e], out_offset=None, in_=peer_v,
                        in_offset=bass.IndirectOffsetOnAxis(ap=idx_fix[:, par * BATCH + e:par * BATCH + e + 1], axis=0),
                    ).then_inc(v_in[e], 16)

            gather(0, 0, True)
            gather(1, 1)
            with pool.Fori(1, TB * BPB // 2) as i:
                for par in range(2):
                    gather(i * 2 + par, par)

        @block.tensor
        def _(pe):
            mm = nc.tensor.matmul

            def unit(i, c, rows, act_t, halves=(0, 1), bank=None, ks=range(KT), inputs=None, cols=UN,
                     side=None, half_done=None):
                slot = c % 4
                w = W[slot] if side is None else pq_side[side]
                bank = PJ[slot] if bank is None else bank
                for n in halves:
                    first = isinstance(i, int) and 4 * i + c == 0
                    if n == 0 and ks[0] == 0 and not first:
                        if side is not None:
                            pe.wait_ge(side_in[side], 16)
                        else:
                            skipped = isinstance(i, int) and 4 * i + c in (U_PQ + 4, U_PQ + 5)
                            pe.wait_ge(w_landed[slot], i * 16 + 16 * (c // 4 + 1 - skipped))
                        if not (isinstance(i, int) and 4 * i + c < 4):
                            pe.wait_ge(evac_done, i * 4 + c - 3)
                    for k in ks if n == halves[0] else range(KT):
                        if inputs and n == 0:
                            inputs(k)
                        if rows:
                            lhs = act_t[:, k * SEQ + n * P:k * SEQ + n * P + P]
                            rhs = w[:, k * UN:k * UN + cols]
                        else:
                            lhs = w[:, k * UN + n * P:k * UN + n * P + P]
                            rhs = act_t[:, k * SEQ:(k + 1) * SEQ]
                        ins = mm(bank[:, n * 256:n * 256 + rhs.shape[1]], lhs, rhs, start=k == 0, stop=k == KT - 1)
                    if n == 1:
                        ins.then_inc(proj_done, 1)
                    elif half_done is not None:
                        ins.then_inc(half_done, 1)

            def unit_begun(c, rows, act_t, ready):
                unit(0, c, rows, act_t, (0,), ks=range(ready))

            def unit_rest(c, rows, act_t, ready):
                unit(0, c, rows, act_t, (0, 1), ks=range(ready, KT))

            def transpose(dst, src):
                return nc.tensor.transpose(dst, src, ident)

            def first_pieces(k):
                if k % (KT // PIECES) == 0:
                    piece = k // (KT // PIECES)
                    pe.wait_ge(x_in[piece], 16)
                    pe.wait_ge(w_landed[0] if piece == PIECES - 1 else w0_in[piece], 16)

            unit(0, U_CKV, True, xt, inputs=first_pieces)
            unit(0, U_IK, True, xt, cols=IK_COLS)

            def hg_scores(p):
                pe.wait_ge(qk_ready, p * 4 + 4)
                for g in range(4):
                    ins = transpose(B[0][:, g * P:(g + 1) * P], a_pr[:, 1536 + g * P:1536 + (g + 1) * P])
                ins.then_inc(kd_ps, 1)
                for g in range(4):
                    ins = mm(B[1][:, g * P:(g + 1) * P], a_pr[:, 512 + g * P:512 + (g + 1) * P], a_pr[:, g * P:(g + 1) * P],
                             start=True, stop=True)
                ins.then_inc(at_ps, 1)

            def hg_updates(p):
                pe.wait_ge(kd_sb, p + 1)
                pe.wait_ge(evac_done, p * 4 + U_HG + 3)
                for h in range(2):
                    for c in range(NCH - 1):
                        g, r = h * 2 + c // 2, (c % 2) * CHUNK
                        ins = mm(update(c, h), a_kd[r:r + CHUNK, g * P:(g + 1) * P],
                                 a_v[r:r + CHUNK, (c // 2) * 256 + h * P:(c // 2) * 256 + (h + 1) * P], start=True, stop=True)
                ins.then_inc(u_ps, 1)

            def hg_out(p):
                pe.wait_ge(at_sb, p + 1)
                pe.wait_ge(st_sb, p + 1)
                for h in range(2):
                    for tb in range(TB):
                        o = h * 256 + tb * P
                        ins = mm(B[0][:, o:o + P], a_v[:, tb * 256 + h * P:tb * 256 + (h + 1) * P],
                                 a_at[:, (h * 2 + tb) * P:(h * 2 + tb + 1) * P], start=True, stop=True, skip_group_check=True)
                        for c in (2 * tb, 2 * tb + 1):
                            if c:
                                o = h * 256 + c * CHUNK
                                ins = mm(B[0][:, o:o + CHUNK], a_st[:, h * 384 + (c - 1) * P:h * 384 + c * P],
                                         a_pr[:, 1024 + o:1024 + o + CHUNK], start=False, stop=True, skip_group_check=True)
                ins.then_inc(ot_ps, 1)

            def hg_mean(p):
                pe.wait_ge(sq_sb, p + 1)
                for h in range(2):
                    cols = slice(h * 256, (h + 1) * 256)
                    ins = mm(B[1][:, cols], mean_m, a_sq[:, cols], start=True, stop=True)
                ins.then_inc(ms_ps, 1)

            hg_steps = (hg_scores, hg_updates, hg_out, hg_mean)

            def hg_body(p):
                for n in range(4):
                    rows = n == 2
                    unit(p, U_HG + n, rows, xt)
                    hg_steps[n](p - 1)

            for n in range(3):
                unit(0, U_HG + n, n == 2, xt)
            pe.wait_ge(rb_in, 32)
            mm(B[3][0:16, 0:384], oh[0:32, 384:400], oh[0:32, 0:384], start=True, stop=True).then_inc(rb_ps, 1)
            pe.wait_ge(const_in, 16)
            pe.wait_ge(cn_done, 4)
            for rc in range(2):
                for tb in range(TB):
                    transpose(B[0][:, rc * 256 + tb * P:rc * 256 + (tb + 1) * P], cn[:, tb * 256 + rc * P:tb * 256 + (rc + 1) * P])
            for tb in range(TB):
                ins = transpose(B[1][:, tb * P:(tb + 1) * P], ikw[:, tb * 256:tb * 256 + P])
            ins.then_inc(cn_ps, 1)
            unit(0, U_HG + 3, False, xt)
            pe.wait_ge(cn_sb, 2)
            with pe.Fori(1, PAIRS) as p:
                hg_body(p)

            pe.wait_ge(mem_in, 16)
            for j in range(UPM):
                unit(8, U_CK - 32 + j, False, mem_a)
                if j < 4:
                    hg_steps[j](PAIRS - 1)

            def index_scores(j):
                pe.wait_ge(evac_done, U_IQ + j + 1)
                if j >= 2:
                    pe.wait_ge(relu_sb, j - 1)
                elif j == 0:
                    pe.wait_ge(oh_done, 2 * PAIRS)
                for h in range(2):
                    bank = B[2 * (j % 2) + h]
                    q = iq[j % 2][:, h * 256:(h + 1) * 256]
                    mm(bank[:, 0:256], q[:, P:256], ik_t, start=True, stop=True)
                    ins = mm(bank[:, 256:384], q[:, 0:P], ik_t[:, 0:P], start=True, stop=True)
                ins.then_inc(sidx_ps, 1)

            for j in range(UPM):
                unit(0, U_IQ + j, False, xt)
                if j:
                    index_scores(j - 1)
            index_scores(UPM - 1)

            with pe.Fori(0, UPM // 2) as it:
                for n in range(4):
                    unit(it + U_GA // 4, U_GA % 4 + n, False, xt if n % 2 == 0 else oh)

            def keys_values(j, par, turn):
                pe.wait_ge(ukv_in[par], turn * 16 + 16)
                if isinstance(j, int) and j == 0:
                    pe.wait_ge(relu_sb, UPM)
                else:
                    pe.wait_ge(ob_sb, j)
                    pe.wait_ge(kv_sb, j * 2)
                for h in range(2):
                    for rc in range(2):
                        mm(B[0][:, h * 256:(h + 1) * 256], wukv[par][:, rc * 256 + h * P:rc * 256 + (h + 1) * P],
                           ckv_t[:, rc * 256:(rc + 1) * 256], start=rc == 0, stop=rc == 1)
                for sb in range(TB):
                    for rc in range(2):
                        ins = mm(B[1][:, sb * 256:(sb + 1) * 256], ckv_t[:, rc * 256 + sb * P:rc * 256 + (sb + 1) * P],
                                 wukv[par][:, 512 + rc * 256:512 + (rc + 1) * 256], start=rc == 0, stop=rc == 1)
                ins.then_inc(kv_ps, 1)

            def logits(j, par):
                pe.wait_ge(kv_sb, j * 2 + 2)
                pe.wait_ge(evac_done, j * 2 + U_AQ + 1)
                if not (isinstance(j, int) and j == 0):
                    pe.wait_ge(pt_sb, j)
                for h in range(2):
                    q = aq[par][:, h * 256:(h + 1) * 256]
                    mm(B[2 + h][:, 0:256], q[:, P:256], khs[:, h * 256:(h + 1) * 256], start=True, stop=True)
                    ins = mm(B[2 + h][:, 256:384], q[:, 0:P], khs[:, h * 256:h * 256 + P], start=True, stop=True)
                ins.then_inc(lg_ps, 1)

            def turn_probs(j):
                pe.wait_ge(p_ready, j * 2 + 2)
                for h in range(2):
                    for c in range(3):
                        ins = transpose(B[2 + h][:, c * P:(c + 1) * P], lg[:, h * 384 + c * P:h * 384 + (c + 1) * P])
                ins.then_inc(pt_ps, 1)

            def attend(j):
                pe.wait_ge(pt_sb, j + 1)
                for h in range(2):
                    v = [vhs[:, sb * 256 + h * P:sb * 256 + (h + 1) * P] for sb in range(TB)]
                    pr = pt[:, h * 384:(h + 1) * 384]
                    mm(B[0][:, h * 256:h * 256 + P], v[0], pr[:, 256:384], start=True, stop=True)
                    mm(B[0][:, h * 256 + P:(h + 1) * 256], v[0], pr[:, 0:P], start=True, stop=False)
                    ins = mm(B[0][:, h * 256 + P:(h + 1) * 256], v[1], pr[:, P:256], start=False, stop=True)
                ins.then_inc(ob_ps, 1)

            def sparse_body(i, c, j, par, turn):
                unit(i, c, False, xt, (0,))
                keys_values(j - 1, par, turn)
                unit(i, c, False, xt, (1,))
                logits(j - 1, par)
                unit(i, c + 1, False, xt, (0,))
                turn_probs(j - 1)
                unit(i, c + 1, False, xt, (1,))
                attend(j - 1)

            ia, ca = U_AQ // 4, U_AQ % 4
            unit(ia, ca, False, xt)
            unit(ia, ca + 1, False, xt)
            sparse_body(ia, ca + 2, 1, 0, 0)
            with pe.Fori(0, PAIRS // 2 - 1) as it:
                sparse_body(it + ia, ca + 4, it * 2 + 2, 1, it)
                sparse_body(it + ia, ca + 6, it * 2 + 3, 0, it + 1)
            early = 2 * (PAIRS - 1)
            keys_values(PAIRS - 1, 1, PAIRS // 2 - 1)
            unit_begun(U_WB, False, ob_t, early)
            logits(PAIRS - 1, 1)
            unit_begun(U_WB + 1, False, ob_t, early)
            turn_probs(PAIRS - 1)
            unit_begun(U_WB + 2, False, ob_t, early)
            attend(PAIRS - 1)

            pe.wait_ge(ob_sb, PAIRS)
            for n in range(3):
                unit_rest(U_WB + n, False, ob_t, early)
            unit(0, U_WB + 3, False, ob_t)
            with pe.Fori(1, UPM // 4) as it:
                for n in range(4):
                    unit(it + U_WB // 4, U_WB % 4 + n, False, ob_t)

            def merged(k):
                if k == 0:
                    pe.wait_ge(mixb_done, UPM + 1)
                elif k == KT - 2:
                    pe.wait_ge(mixb_done, UPM + 2)

            unit(0, U_MIX, True, mix_t, inputs=merged)
            for n in range(1, 4):
                unit(0, U_MIX + n, True, mix_t)
            with pe.Fori(1, UPM // 4) as it:
                for n in range(4):
                    unit(it + U_MIX // 4, U_MIX % 4 + n, True, mix_t)

            def turn_h(q, turn):
                tb, k4 = q // 4, q % 4
                if turn:
                    pe.wait_ge(unit_var, q + 1)
                else:
                    pe.wait_ge(h_done, tb + 1)
                    if q >= 4:
                        pe.wait_ge(tr_sb, q - 3)
                for k in range(4):
                    ins = transpose(B[q % 4][:, k * P:(k + 1) * P],
                                    h_tok[:, tb * D + (4 * k4 + k) * P:tb * D + (4 * k4 + k + 1) * P])
                ins.then_inc(tr_ps, 1)

            pe.wait_ge(mem_in, 32)
            for j in range(UPM):
                unit(0, U_CV + j, True, mem_b)
                if j >= 4:
                    for q in (2 * (j - 4), 2 * (j - 4) + 1):
                        turn_h(q, 0)

            def cross_logits(m):
                pe.wait_ge(evac_done, U_CQ + 2 * m + 2)
                if m:
                    pe.wait_ge(ce_done, 2 * m)
                for tb in range(TB):
                    for c in range(4):
                        ins = mm(B[0][:, tb * 256:(tb + 1) * 256], qc[m % 2][:, c * 256 + tb * P:c * 256 + (tb + 1) * P],
                                 kc_t[:, (4 * m + c) * 256:(4 * m + c + 1) * 256], start=c == 0, stop=c == 3)
                ins.then_inc(cl_ps, 1)

            def cross_turn(m):
                pe.wait_ge(cp_done, 2 * m + 2)
                if m:
                    pe.wait_ge(ct_sb, m)
                for mb in range(2):
                    for tb in range(TB):
                        ins = transpose(B[1][:, mb * 256 + tb * P:mb * 256 + (tb + 1) * P],
                                        pc[:, tb * 256 + mb * P:tb * 256 + (mb + 1) * P])
                ins.then_inc(ct_ps, 1)

            def cross_out(m):
                pe.wait_ge(ct_sb, m + 1)
                if m:
                    pe.wait_ge(co_sb, m)
                for c in range(4):
                    for mb in range(2):
                        ins = mm(B[2 + c // 2][:, (c % 2) * 256:(c % 2 + 1) * 256],
                                 vc[:, mb * D + m * MEM_DH + c * P:mb * D + m * MEM_DH + (c + 1) * P],
                                 ptc[:, mb * 256:(mb + 1) * 256], start=mb == 0, stop=mb == 1)
                ins.then_inc(co_ps, 1)

            def turned(k):
                if k % 4 == 0:
                    pe.wait_ge(tr_sb, 4 + k // 4 + 1)

            for m in range(MEM_HEADS):
                unit(0, U_CQ + 2 * m, False, h_t, (0,), inputs=None if m else turned)
                if m:
                    cross_logits(m - 1)
                unit(0, U_CQ + 2 * m, False, h_t, (1,))
                if m:
                    cross_turn(m - 1)
                unit(0, U_CQ + 2 * m + 1, False, h_t, (0,))
                if m:
                    cross_out(m - 1)
                unit(0, U_CQ + 2 * m + 1, False, h_t, (1,))
            early = 4 * (MEM_HEADS - 1)
            cross_logits(MEM_HEADS - 1)
            pe.wait_ge(co_sb, MEM_HEADS - 1)
            unit_begun(U_CO, True, oc_t, early)
            cross_turn(MEM_HEADS - 1)
            unit_begun(U_CO + 1, True, oc_t, early)
            cross_out(MEM_HEADS - 1)
            unit_begun(U_CO + 2, True, oc_t, early)
            pe.wait_ge(co_sb, MEM_HEADS)
            for n in range(3):
                unit_rest(U_CO + n, True, oc_t, early)
            for n in range(3, UPM - 1):
                unit(0, U_CO + n, True, oc_t)
            unit(0, U_PQ - 1, True, oc_t, (0,), half_done=last0_ps)
            pe.wait_ge(evac_done, U_PQ - 2)
            unit(0, U_PQ - 1, True, oc_t, (1,), bank=PJ[3])

            def sum_rows(b, Y, last=False):
                for e in range(BATCH):
                    pe.wait_ge(diag_done, b * BATCH + e + 1)
                    pe.wait_ge(v_in[e], b * 16 + 16)
                    for c in range(4):
                        ins = mm(Y[c], diag[:, e * P:(e + 1) * P], v_rows[e][:, c * 512:(c + 1) * 512],
                                 start=False, stop=True, skip_group_check=True)
                        if last and e == BATCH - 1:
                            ins.then_inc(bank_done, 1)
                    if not (last and e == BATCH - 1):
                        ins.then_inc(v_used, 1)

            def residual(tb, Y):
                for c in range(4):
                    mm(Y[c], C[:, K_ALPHA:K_ALPHA + P], h_tok[:, tb * D + c * 512:tb * D + (c + 1) * 512],
                       start=True, stop=True, skip_group_check=True)

            def key_products(bank, at, tb, k):
                for h in range(2):
                    ins = mm(bank[:, at + h * P:at + (h + 1) * P], qp[:, h * 256 + tb * P:h * 256 + (tb + 1) * P],
                             keys_t[:, (2 * k + h) * P:(2 * k + h + 1) * P], start=True, stop=True)
                return ins

            def first_queries(tb):
                for k in range(KT):
                    if k % 4 == 0:
                        q = 4 * tb + k // 4
                        if tb == 0 and q % 2:
                            pe.wait_ge(tv_sb, q // 2 + 1)
                        else:
                            pe.wait_ge(tr_sb, 8 + (q // 2 + 1 if tb == 0 else q - 1))
                    for n in range(2):
                        ins = mm(PJ[n][:, 0:P], pq_side[0][:, k * UN + n * P:k * UN + (n + 1) * P],
                                 h_t[:, k * SEQ + tb * P:k * SEQ + (tb + 1) * P], start=k == 0, stop=k == KT - 1)
                return ins

            def peer_scores(k):
                unit(0, U_PQ + k, False, h_t, bank=PJ[(k + 1) % 2], side=1 if k == 1 else None)
                pe.wait_ge(evac_done, U_PQ + k + 1)
                pe.wait_ge(psc_sb, k)
                for tb in range(TB):
                    ins = key_products(PJ[2 + (k + 1) % 2], tb * 256, tb, k)
                ins.then_inc(psc_ps, 1)

            for q in range(4):
                turn_h(q, 1)
            pe.wait_ge(side_in[0], 16)
            first_queries(0).then_inc(q0_ps, 1)
            turn_h(4, 1)
            pe.wait_ge(keys_in, 16)
            pe.wait_ge(q0_sb, 1)
            key_products(PJ[2], 0, 0, 0).then_inc(psc_ps, 1)
            for q in range(5, 8):
                turn_h(q, 1)
            first_queries(1).then_inc(proj_done, 1)
            pe.wait_ge(evac_done, U_PQ + 1)
            key_products(PJ[3], 0, 1, 0).then_inc(psc_ps, 1)
            peer_scores(1)
            pe.wait_ge(tr_sb, 14)
            pe.wait_ge(h_final[0], 1)
            residual(0, B)
            for n in range(1, 2 * PEER_HEADS):
                if n % 2 and (n + 3) // 2 < PEER_HEADS:
                    peer_scores((n + 3) // 2)
                sum_rows(n - 1, B)
            with pe.Fori(EARLY, BPB) as b:
                sum_rows(b, B)
            pe.wait_ge(psc_sb, PEER_HEADS + 1)
            pe.wait_ge(h_final[1], 1)
            residual(1, PJ)
            with pe.Fori(BPB, TB * BPB - 1) as b:
                sum_rows(b, PJ)
            sum_rows(TB * BPB - 1, PJ, True)

        @block.scalar
        def _(act):
            chain = Chain(act, act_chain)
            fn = nc.scalar.activation

            def mark(ins, s, value):
                ins.then_inc(s, 1)
                act.wait_ge(s, value)

            act.wait_ge(proj_done, U_CKV + 1)
            mark(fn(ckv, PJ[U_CKV], ACT.Copy), evac_done, U_CKV + 1)
            act.wait_ge(proj_done, U_IK + 1)
            mark(fn(ikw.rearrange("p (b n) -> p b n", b=2)[:, :, 0:IK_COLS],
                    PJ[U_IK].rearrange("p (b n) -> p b n", b=2)[:, :, 0:IK_COLS], ACT.Copy), evac_done, U_IK + 1)
            act.wait_ge(lbd_done, 1)
            mark(fn(lbr, lbr, ACT.Exp), lbe_done, 1)
            for tb in range(TB):
                mark(fn(cn[:, tb * 256:(tb + 1) * 256], ckv[:, tb * 256:(tb + 1) * 256], ACT.Square,
                        accum_out=ss[:, tb:tb + 1]), ss_done, tb + 1)
            act.wait_ge(eps_set, 2)
            act.wait_ge(mv_done, 2)
            chain.link(fn(rs, ss, ACT.Ln, scale=1.0 / 256, bias=eps_rms))
            mark(fn(rs, rs, ACT.Exp, scale=-0.5), rn_done, 1)
            chain.link(fn(g2, mv[:, 1:4:2], ACT.Ln, bias=eps_ln))
            mark(fn(g2, g2, ACT.Exp, scale=-0.5), rn_done, 2)

            def hg_body(p, new, old):
                zero = isinstance(p, int) and p == 0
                u = p * 4 + U_HG
                if new:
                    act.wait_ge(proj_done, u + 1)
                    if not zero:
                        act.wait_ge(f_ready, p)
                    mark(fn(a_sf, PJ[U_HG % 4], ACT.Sigmoid), evac_done, u + 1)
                if old:
                    act.wait_ge(kd_ps, p)
                    mark(fn(a_kd, B[0], ACT.Copy), kd_sb, p)
                if new:
                    act.wait_ge(proj_done, u + 2)
                    if not zero:
                        act.wait_ge(qk_ready, p * 4)
                    mark(fn(a_q, PJ[(U_HG + 1) % 4], ACT.Copy), evac_done, u + 2)
                    act.wait_ge(proj_done, u + 3)
                    if not zero:
                        act.wait_ge(ot_ps, p)
                    mark(fn(a_v, PJ[(U_HG + 2) % 4], ACT.Copy), evac_done, u + 3)
                if old:
                    act.wait_ge(ot_ps, p)
                    act.wait_ge(f_ready, p + 1)
                    mark(fn(a_sq, B[0], ACT.Square), sq_sb, p)
                if zero:
                    act.wait_ge(rb_ps, 1)
                    mark(fn(oh[0:16, 512:896], B[3][0:16, 0:384], ACT.Copy), rb_sb, 1)
                    act.wait_ge(cn_ps, 1)
                    mark(fn(ckv_t, B[0], ACT.Copy), cn_sb, 1)
                    mark(fn(ik_t, B[1][:, 0:256], ACT.Copy), cn_sb, 2)
                if new:
                    act.wait_ge(proj_done, u + 4)
                    if not zero:
                        act.wait_ge(t2_done, p)
                    mark(fn(a_sg, PJ[(U_HG + 3) % 4], ACT.Sigmoid), gate_rd, p + 1)
                    mark(fn(a_gr, PJ[(U_HG + 3) % 4], ACT.Copy), evac_done, u + 4)
                    act.wait_ge(f_ready, p + 1)
                    mark(fn(a_f, a_f, ACT.Ln), lf_ready, p + 1)
                if old:
                    act.wait_ge(ms_ps, p)
                    chain.link(fn(a_sq, B[1], ACT.Ln, bias=eps_rms))
                    mark(fn(a_sq, a_sq, ACT.Exp, scale=-0.5), rs_sb, p)
                if new:
                    act.wait_ge(g_ready, p + 1)
                    if not zero:
                        act.wait_ge(st_sb, p)
                    for n, (src, scale) in enumerate(((a_gd, 1.0), (a_gd, -1.0), (a_g, 1.0), (a_gl, 1.0))):
                        mark(fn(a_ex[:, n * 512:(n + 1) * 512], src, ACT.Exp, scale=scale), ex_ready, p * 4 + n + 1)

            hg_body(0, True, False)
            with act.Fori(1, PAIRS) as p:
                chain.loop(p - 1, 1)
                hg_body(p, True, True)
                chain.end(PAIRS - 1)

            def keys_out(j):
                act.wait_ge(proj_done, U_CK + j + 1)
                mark(fn(kc_t[:, j * 512:(j + 1) * 512], PJ[(U_CK + j) % 4], ACT.Copy), evac_done, U_CK + j + 1)

            keys_out(0)
            act.wait_ge(kd_ps, PAIRS)
            mark(fn(a_kd, B[0], ACT.Copy), kd_sb, PAIRS)
            keys_out(1)
            keys_out(2)
            act.wait_ge(ot_ps, PAIRS)
            act.wait_ge(oh_done, 2 * PAIRS - 2)
            mark(fn(a_sq, B[0], ACT.Square), sq_sb, PAIRS)
            keys_out(3)
            act.wait_ge(ms_ps, PAIRS)
            chain.link(fn(a_sq, B[1], ACT.Ln, bias=eps_rms))
            mark(fn(a_sq, a_sq, ACT.Exp, scale=-0.5), rs_sb, PAIRS)
            for j in range(4, UPM):
                keys_out(j)

            def relu_out(j):
                act.wait_ge(sidx_ps, j + 1)
                if j >= 2:
                    act.wait_ge(acc_done, j - 1)
                banks = PS[:, 4 + 2 * (j % 2):6 + 2 * (j % 2), 0:384]
                mark(fn(relu[j % 2].rearrange("p (h x) -> p h x", h=2), banks, ACT.Relu, scale=IDX_DIM ** -0.5), relu_sb, j + 1)

            for j in range(UPM):
                act.wait_ge(proj_done, U_IQ + j + 1)
                if j >= 2:
                    act.wait_ge(sidx_ps, j - 1)
                mark(fn(iq[j % 2], PJ[(U_IQ + j) % 4], ACT.Copy), evac_done, U_IQ + j + 1)
                if j:
                    relu_out(j - 1)
            relu_out(UPM - 1)

            with act.Fori(0, UPM // 2) as it:
                for n in range(2):
                    u = it * 4 + U_GA + 2 * n
                    act.wait_ge(proj_done, u + 1)
                    act.wait_ge(mixa_done, it * 2 + n + 1)
                    mark(fn(ga[n], PJ[(U_GA + 2 * n) % 4], ACT.Sigmoid), evac_done, u + 1)
                    act.wait_ge(proj_done, u + 2)
                    mark(fn(yb[n], PJ[(U_GA + 2 * n + 1) % 4], ACT.Copy), evac_done, u + 2)

            def kv_out(j):
                act.wait_ge(kv_ps, j + 1)
                if not (isinstance(j, int) and j == 0):
                    act.wait_ge(lg_ps, j)
                mark(fn(khs, B[0], ACT.Copy), kv_sb, j * 2 + 1)
                if not (isinstance(j, int) and j == 0):
                    act.wait_ge(ob_ps, j)
                mark(fn(vhs, B[1], ACT.Copy), kv_sb, j * 2 + 2)

            def exps(j):
                act.wait_ge(lg_rd, j + 1)
                for g in range(4):
                    h, tb = g // 2, g % 2
                    cols = lg[:, h * 384:h * 384 + 256] if tb == 0 else lg[:, h * 384 + 256:(h + 1) * 384]
                    mark(fn(cols, cols, ACT.Exp, bias=nmax[:, g:g + 1], accum_out=esum[:, g:g + 1]), p_exp, j * 4 + g + 1)

            def probs_out(j):
                act.wait_ge(pt_ps, j + 1)
                if not (isinstance(j, int) and j == 0):
                    act.wait_ge(ob_ps, j)
                mark(fn(pt.rearrange("p (h x) -> p h x", h=2), B23[:, :, 0:384], ACT.Copy), pt_sb, j + 1)

            def attended_out(j):
                act.wait_ge(ob_ps, j + 1)
                mark(fn(ob_t[:, bass.ds(j * 512, 512)], B[0], ACT.Copy), ob_sb, j + 1)

            def q_out(j, bank, par):
                act.wait_ge(proj_done, j * 2 + U_AQ + 1)
                if not (isinstance(j, int) and j < 2):
                    act.wait_ge(lg_ps, j - 1)
                mark(fn(aq[par], bank, ACT.Copy, scale=AT_DH ** -0.5), evac_done, j * 2 + U_AQ + 1)

            def gate_out(j, bank):
                act.wait_ge(proj_done, j * 2 + U_AQ + 2)
                mark(fn(gate_b[:, bass.ds(j * 512, 512)], bank, ACT.Sigmoid), evac_done, j * 2 + U_AQ + 2)

            def sparse_body(j, c, par):
                kv_out(j - 1)
                q_out(j, PJ[c % 4], par)
                exps(j - 1)
                probs_out(j - 1)
                gate_out(j, PJ[(c + 1) % 4])
                attended_out(j - 1)

            q_out(0, PJ[U_AQ % 4], 0)
            gate_out(0, PJ[(U_AQ + 1) % 4])
            sparse_body(1, U_AQ + 2, 1)
            with act.Fori(0, PAIRS // 2 - 1) as it:
                sparse_body(it * 2 + 2, U_AQ + 4, 0)
                sparse_body(it * 2 + 3, U_AQ + 6, 1)
            kv_out(PAIRS - 1)
            exps(PAIRS - 1)
            probs_out(PAIRS - 1)
            attended_out(PAIRS - 1)

            with act.Fori(0, UPM // 4) as it:
                for n in range(4):
                    u = it * 4 + U_WB + n
                    act.wait_ge(proj_done, u + 1)
                    act.wait_ge(mixb_done, it * 4 + n + 1)
                    mark(fn(yb[n % 2], PJ[(U_WB + n) % 4], ACT.Copy), evac_done, u + 1)

            def rows_out(first, z_before, n):
                act.wait_ge(proj_done, first + n + 1)
                act.wait_ge(z_done, n + z_before + 1)
                mark(fn(yz[n % 2], PJ[(first + n) % 4], ACT.Copy), evac_done, first + n + 1)

            for n in range(UPM):
                rows_out(U_MIX, 0, n)

            def rstd(tb):
                act.wait_ge(lnv_done, tb + 1)
                chain.link(fn(rs[:, tb:tb + 1], mv[:, 2 * tb + 1:2 * tb + 2], ACT.Ln, bias=eps_ln))
                mark(fn(rs[:, tb:tb + 1], rs[:, tb:tb + 1], ACT.Exp, scale=-0.5), lnr_done, tb + 1)

            def turned_out(q):
                tb, k4 = q // 4, q % 4
                act.wait_ge(tr_ps, q + 1)
                dst = h_t.rearrange("p (k t) -> p k t", k=KT)[:, 4 * k4:4 * k4 + 4, tb * P:(tb + 1) * P]
                mark(fn(dst, B[q % 4].rearrange("p (k t) -> p k t", k=4), ACT.Copy), tr_sb, q + 1)

            rstd(0)
            for j in range(UPM):
                act.wait_ge(proj_done, U_CV + j + 1)
                dst = vc.rearrange("p (b n) -> p b n", b=2)[:, :, j * UN:(j + 1) * UN]
                mark(fn(dst, PJ[(U_CV + j) % 4].rearrange("p (b n) -> p b n", b=2), ACT.Copy), evac_done, U_CV + j + 1)
                if j == 0:
                    rstd(1)
                if j >= 4:
                    for q in (2 * (j - 4), 2 * (j - 4) + 1):
                        turned_out(q)

            def cross_exps(m):
                act.wait_ge(cl_rd, m + 1)
                for tb in range(TB):
                    if m:
                        act.wait_ge(ct_ps, m)
                    mark(fn(pc[:, tb * 256:(tb + 1) * 256], B[0][:, tb * 256:(tb + 1) * 256], ACT.Exp, scale=MEM_DH ** -0.5,
                            bias=nmax[:, tb:tb + 1], accum_out=esum[:, tb:tb + 1]), ce_done, 2 * m + tb + 1)

            def cross_turned(m):
                act.wait_ge(ct_ps, m + 1)
                if m:
                    act.wait_ge(co_ps, m)
                mark(fn(ptc, B[1], ACT.Copy), ct_sb, m + 1)

            def cross_attended(m):
                act.wait_ge(co_ps, m + 1)
                mark(fn(oc_t[:, m * 1024:(m + 1) * 1024].rearrange("p (a b) -> p a b", a=2), B23, ACT.Copy), co_sb, m + 1)

            def cq_out(m, n):
                u = U_CQ + 2 * m + n
                act.wait_ge(proj_done, u + 1)
                if m >= 2:
                    act.wait_ge(cl_ps, m - 1)
                mark(fn(qc[m % 2][:, n * 512:(n + 1) * 512], PJ[u % 4], ACT.Copy), evac_done, u + 1)

            for m in range(MEM_HEADS):
                if m:
                    cross_exps(m - 1)
                cq_out(m, 0)
                if m:
                    cross_turned(m - 1)
                    cross_attended(m - 1)
                cq_out(m, 1)
            cross_exps(MEM_HEADS - 1)
            cross_turned(MEM_HEADS - 1)
            cross_attended(MEM_HEADS - 1)

            for n in range(UPM - 1):
                rows_out(U_CO, UPM, n)

            def root_ready(turn_tb, cols):
                act.wait_ge(lnv_done, turn_tb)
                mark(fn(cols, cols, ACT.Sqrt, bias=eps_ln), lnr_done, turn_tb)

            def load_root():
                chain.link(fn(warm, eps_ln, ACT.Sqrt))

            load_root()
            last = yz[(UPM - 1) % 2]
            act.wait_ge(last0_ps, 1)
            act.wait_ge(z_done, 2 * UPM)
            mark(fn(last[:, 0:256], PJ[(U_PQ - 1) % 4][:, 0:256], ACT.Copy), last0_sb, 1)
            root_ready(3, mv[:, 1:2])
            act.wait_ge(proj_done, U_PQ)
            mark(fn(last[:, 256:512], PJ[3][:, 256:512], ACT.Copy), evac_done, U_PQ)

            def turned_scaled(q):
                tb, k4 = q // 4, q % 4
                act.wait_ge(tr_ps, 8 + q + 1)
                for k in range(4):
                    f = 4 * k4 + k
                    ins = fn(h_t[:, f * SEQ + tb * P:f * SEQ + (tb + 1) * P], B[q % 4][:, k * P:(k + 1) * P], ACT.Identity,
                             scale=ln2_g[:, f:f + 1], bias=ln2_b[:, f:f + 1])
                ins.then_inc(tr_sb, 1)

            act.wait_ge(ln2c_in, 16)
            for q in (0, 2):
                turned_scaled(q)
            root_ready(4, mv[:, 3:4])

            def step(b, first=False):
                for e in range(BATCH):
                    act.wait_ge(dot_done, b * BATCH + e + 1)
                    if not first:
                        act.wait_ge(v_used, b * BATCH + e - BATCH + 1)
                    chain.link(fn(hg4[:, e:e + 1], dots[:, e:e + 1], ACT.Gelu))
                    mark(fn(gh4[:, e:e + 1], gates[:, bass.ds(b * BATCH + e, 1)], ACT.Copy, scale=hg4[:, e:e + 1]),
                         gh_done, b * BATCH + e + 1)
                    mark(fn(diag[:, e * P:(e + 1) * P], ident, ACT.Copy, scale=gh4[:, e:e + 1]), diag_done, b * BATCH + e + 1)

            def first_queries_out(tb):
                cols = qp.rearrange("p (h t) -> p h t", h=2)[:, :, tb * P:(tb + 1) * P]
                if tb == 0:
                    act.wait_ge(q0_ps, 1)
                    mark(fn(cols, PS[:, 0:2, 0:P], ACT.Copy), q0_sb, 1)
                else:
                    act.wait_ge(proj_done, U_PQ + 1)
                    mark(fn(cols, PS[:, 0:2, 0:P], ACT.Copy), evac_done, U_PQ + 1)

            def first_scores_out(tb):
                act.wait_ge(psc_ps, tb + 1)
                mark(fn(sc[:, tb * 256:(tb + 1) * 256], PJ[2 + tb][:, 0:256], ACT.Copy), psc_sb, tb + 1)

            def queries_out(k):
                act.wait_ge(proj_done, U_PQ + k + 1)
                act.wait_ge(psc_ps, k + 1)
                mark(fn(qp, PJ[(k + 1) % 2], ACT.Copy), evac_done, U_PQ + k + 1)

            def scores_out(k):
                act.wait_ge(psc_ps, k + 2)
                act.wait_ge(head_done, 2 * k)
                mark(fn(sc, PJ[2 + (k + 1) % 2], ACT.Copy), psc_sb, k + 2)

            def gates_exp(n):
                act.wait_ge(tops_rd, n + 1)
                mark(fn(e_top, e_top, ACT.Exp), gexp_done, n + 1)

            first_queries_out(0)
            first_scores_out(0)
            for q in range(4, 8):
                turned_scaled(q)
            first_queries_out(1)
            first_scores_out(1)
            gates_exp(0)
            queries_out(1)
            for n in range(1, 2 * PEER_HEADS):
                gates_exp(n)
                if n % 2 and (n + 1) // 2 < PEER_HEADS:
                    scores_out((n + 1) // 2)
                if n % 2 and (n + 3) // 2 < PEER_HEADS:
                    queries_out((n + 3) // 2)
                step(n - 1, n == 1)
            with act.Fori(EARLY, BPB) as b:
                chain.loop(b - EARLY, BATCH)
                step(b)
                chain.end(BPB - EARLY)
            step(BPB)
            root_ready(5, mv[:, 1:2])
            with act.Fori(BPB + 1, TB * BPB) as b:
                chain.loop(b - BPB - 1, BATCH)
                step(b)
                chain.end(BPB - 1)
            load_root()
            root_ready(6, mv[:, 3:4])

        @block.vector
        def _(dve):
            chain = Chain(dve, dve_chain)
            v = nc.vector
            link = chain.link

            def mark(ins, s, value):
                ins.then_inc(s, 1)
                dve.wait_ge(s, value)

            dve.wait_ge(row_in, 80)
            link(v.tensor_tensor(lbm, lbr[:, 0:16], lbr[:, 16:32], ALU.max))
            link(v.tensor_tensor(lbr[:, 0:16], lbr[:, 0:16], lbm, ALU.subtract))
            mark(v.tensor_tensor(lbr[:, 16:32], lbr[:, 16:32], lbm, ALU.subtract), lbd_done, 1)
            dve.wait_ge(lbe_done, 1)
            link(v.tensor_tensor(lbm, lbr[:, 0:16], lbr[:, 16:32], ALU.add))
            link(v.reciprocal(lbm, lbm))
            link(v.tensor_tensor(lb, lbr[:, 0:16], lbm, ALU.mult))
            link(v.tensor_scalar(omlb, lb, -1.0, 1.0, ALU.mult, ALU.add))
            link(v.memset(a_at, 0.0))
            dve.wait_ge(evac_done, U_IK + 1)
            for tb in range(TB):
                link(v.bn_stats(stats[:, 6 * tb:6 * tb + 6], ikw[:, tb * 256:tb * 256 + P]))
                mark(v.bn_aggr(mv[:, 2 * tb:2 * tb + 2], stats[:, 6 * tb:6 * tb + 6]), mv_done, tb + 1)
            for tb in range(TB):
                link(v.tensor_scalar(iw[:, tb * 16:(tb + 1) * 16], ikw[:, tb * 256 + P:tb * 256 + P + HEADS],
                                     HEADS ** -0.5, None, ALU.mult))
            dve.wait_ge(ss_done, 2)
            dve.wait_ge(rn_done, 2)
            for tb in range(TB):
                cols = ckv[:, tb * 256:(tb + 1) * 256]
                mark(v.scalar_tensor_tensor(cn[:, tb * 256:(tb + 1) * 256], cols, rs[:, tb:tb + 1], row_kv, ALU.mult, ALU.mult),
                     cn_done, tb + 1)
            for tb in range(TB):
                cols = ikw[:, tb * 256:tb * 256 + P]
                link(v.tensor_scalar(cols, cols, mv[:, 2 * tb:2 * tb + 1], g2[:, tb:tb + 1], ALU.subtract, ALU.mult))
                link(v.tensor_tensor(cols, cols, row_ikg, ALU.mult))
                mark(v.tensor_tensor(cols, cols, row_ikb, ALU.add), cn_done, tb + 3)

            def hg_body(p, new, old):
                if new:
                    dve.wait_ge(evac_done, p * 4 + U_HG + 1)
                    for h in range(2):
                        link(v.tensor_scalar(a_f[:, h * 256:(h + 1) * 256], a_sf[:, h * 256:(h + 1) * 256],
                                             omlb[:, bass.ds(p * 2 + h, 1)], lb[:, bass.ds(p * 2 + h, 1)], ALU.mult, ALU.add))
                    mark(v.tensor_scalar(a_k, a_f, -1.0, 1.0, ALU.mult, ALU.add), f_ready, p + 1)
                if old:
                    dve.wait_ge(at_ps, p)
                    dve.sem_inc(at_seen, 1)
                    mask = C[:, K_AMASK:K_AMASK + P].bitcast(U32).unsqueeze(1).to_broadcast([P, 4, P])
                    mark(v.copy_predicated(a_at.rearrange("p (g i) -> p g i", g=4), mask,
                                           B[1].rearrange("p (g i) -> p g i", g=4)), at_sb, p)
                    dve.wait_ge(u_ps, p)
                    st = a_st.rearrange("p (h c n) -> p h c n", h=2, c=3)
                    link(v.tensor_copy(st[:, :, 0, :], B[2][:, 0:256].rearrange("p (h n) -> p h n", h=2)))
                    for c in (1, 2):
                        for h in range(2):
                            last = 1024 + h * 256 + (c + 1) * CHUNK - 1
                            ins = v.scalar_tensor_tensor(st[:, h, c, :], st[:, h, c - 1, :], a_ex[:, last:last + 1],
                                                         update(c, h), ALU.mult, ALU.add)
                            if (c, h) == (2, 1):
                                mark(ins, st_sb, p)
                            else:
                                link(ins)
                    dve.wait_ge(sq_sb, p)
                    mark(v.tensor_tensor(a_t2, B[0], a_gr, ALU.mult), t2_done, p)
                if new:
                    dve.wait_ge(gate_rd, p + 1)
                    dve.wait_ge(evac_done, p * 4 + U_HG + 4)
                    link(v.tensor_tensor(a_gr, a_gr, a_sg, ALU.mult))
                if old:
                    dve.wait_ge(rs_sb, p)
                    for h in range(2):
                        mark(v.scalar_tensor_tensor(oh[:, bass.ds(p * 512 - 512 + h * 256, 256)], a_t2[:, h * 256:(h + 1) * 256],
                                                    hgn[:, bass.ds(p * 2 - 2 + h, 1)], a_sq[:, h * 256:(h + 1) * 256],
                                                    ALU.mult, ALU.mult), oh_done, p * 2 - 1 + h)
                if new:
                    dve.wait_ge(lf_ready, p + 1)
                    link(v.tensor_tensor_scan(a_g, C[:, K_RESET:K_RESET + 512], a_f, 0.0, ALU.mult, ALU.add))
                    g3 = a_g.rearrange("p (c t) -> p c t", t=CHUNK)
                    mid = g3[:, :, CHUNK // 2 - 1:CHUNK // 2].to_broadcast([P, 8, CHUNK])
                    end = g3[:, :, CHUNK - 1:CHUNK].to_broadcast([P, 8, CHUNK])
                    link(v.tensor_tensor(a_gd.rearrange("p (c t) -> p c t", t=CHUNK), g3, mid, ALU.subtract))
                    mark(v.tensor_tensor(a_gl.rearrange("p (c t) -> p c t", t=CHUNK), end, g3, ALU.subtract), g_ready, p + 1)
                    dve.wait_ge(ex_ready, p * 4 + 4)
                    dve.wait_ge(evac_done, p * 4 + U_HG + 2)
                    for n, src in enumerate((a_q, a_k, a_q, a_k)):
                        mark(v.tensor_tensor(a_pr[:, n * 512:(n + 1) * 512], src, a_ex[:, n * 512:(n + 1) * 512], ALU.mult),
                             qk_ready, p * 4 + n + 1)

            dve.wait_ge(const_in, 16)
            hg_body(0, True, False)
            dve.wait_ge(rb_out, 16)
            with dve.Fori(1, PAIRS) as p:
                chain.loop(p - 1, 9)
                hg_body(p, True, True)
                chain.end(PAIRS - 1)
            hg_body(PAIRS, False, True)
            for s in (mixa_done, mixb_done, z_done):
                mark(v.memset(ga[0][:, 0:1], 0.0), s, 1)
                mark(v.memset(ga[0][:, 0:1], 0.0), s, 2)

            dve.wait_ge(cn_ps, 1)
            dve.wait_ge(relu_sb, 1)
            link(v.memset(score, 0.0))
            for j in range(PAIRS):
                dve.wait_ge(relu_sb, j + 1)
                for h in range(2):
                    for tb, lo, hi in ((1, 0, 256), (0, 256, 384)):
                        w = iw[:, tb * 16 + 2 * j + h:tb * 16 + 2 * j + h + 1]
                        ins = v.scalar_tensor_tensor(score[:, lo:hi], relu[j % 2][:, h * 384 + lo:h * 384 + hi], w, score[:, lo:hi],
                                                     ALU.mult, ALU.add)
                        if (h, tb) == (1, 0):
                            mark(ins, acc_done, j + 1)
                        else:
                            link(ins)
            link(v.tensor_tensor(score, score, C[:, K_CAUS:K_CAUS + 384], ALU.add))
            for lo, hi in ((0, 256), (256, 384)):
                with dve.Fori(0, TOPK // 8) as r:
                    chain.loop(r, 2)
                    link(v.max(m8, score[:, lo:hi]))
                    dve.sem_inc(max_seen, 1)
                    link(v.match_replace(score[:, lo:hi], m8, score[:, lo:hi], TAKEN))
                    chain.end(TOPK // 8)
            link(v.tensor_scalar(sel_mask, score, TAKEN / 2, MASKED, ALU.is_gt, ALU.mult))
            mark(v.tensor_tensor(sel_mask, sel_mask, C[:, K_CAUS:K_CAUS + 384], ALU.add), sel_done, 1)

            with dve.Fori(0, UPM // 2) as it:
                for n in range(2):
                    dve.wait_ge(evac_done, it * 4 + U_GA + 2 * n + 2)
                    mark(v.tensor_tensor(mix_t[:, bass.ds(it * 1024 + n * 512, 512)], ga[n], yb[n], ALU.mult),
                         mixa_done, it * 2 + n + 3)

            lg3 = lg.rearrange("p (h x) -> p h x", h=2)
            bias3 = biases.rearrange("p (h x) -> p h x", h=2)
            wide, narrow = slice(0, 256), slice(256, 384)

            def next_biases(j):
                rel = th[:, bass.ds(j * 512, 512)].rearrange("p (h x) -> p h x", h=2)
                for cols, x in ((wide, rel), (narrow, rel[:, :, P:256])):
                    link(v.tensor_tensor(bias3[:, :, cols], x, sel_mask[:, cols].unsqueeze(1).to_broadcast([P, 2, x.shape[2]]), ALU.add))

            def biased(j):
                dve.wait_ge(lg_ps, j + 1)
                if not (isinstance(j, int) and j == 0):
                    dve.wait_ge(pt_ps, j)
                link(v.tensor_tensor(lg3, B23[:, :, 0:384], bias3, ALU.add))
                least = nmax.rearrange("p (h t) -> p h t", h=2)
                link(v.tensor_reduce(least[:, :, 0], lg3[:, :, wide], AX.X, ALU.max, negate=True))
                mark(v.tensor_reduce(least[:, :, 1], lg3[:, :, narrow], AX.X, ALU.max, negate=True), lg_rd, j + 1)

            def normed(j):
                dve.wait_ge(p_exp, j * 4 + 4)
                link(v.reciprocal(rec, esum))
                for n, cols in enumerate((wide, narrow)):
                    r = rec.rearrange("p (h t) -> p h t", h=2)[:, :, n:n + 1].to_broadcast([P, 2, cols.stop - cols.start])
                    mark(v.tensor_tensor(lg3[:, :, cols], lg3[:, :, cols], r, ALU.mult), p_ready, j * 2 + n + 1)

            dve.wait_ge(th_in, 16)
            next_biases(0)
            biased(0)
            normed(0)
            next_biases(1)
            with dve.Fori(1, PAIRS - 1) as j:
                chain.loop(j - 1, 5)
                biased(j)
                normed(j)
                next_biases(j + 1)
                chain.end(PAIRS - 2)
            biased(PAIRS - 1)
            normed(PAIRS - 1)

            with dve.Fori(0, UPM // 2) as it:
                chain.loop(it, 2)
                for n in range(2):
                    dve.wait_ge(evac_done, it * 2 + n + U_WB + 1)
                    cols = mix_t[:, bass.ds(it * 1024 + n * 512, 512)]
                    link(v.tensor_tensor(yb[n], gate_b[:, bass.ds(it * 1024 + n * 512, 512)], yb[n], ALU.mult))
                    mark(v.tensor_tensor(cols, cols, yb[n], ALU.add), mixb_done, it * 2 + n + 3)
                chain.end(UPM // 2)

            def add_residual(n, tb, unit):
                cols = h_tok[:, bass.ds(unit * 256 + tb * D, 256)]
                link(v.scalar_tensor_tensor(cols, cols, ALPHA, yz[n][:, tb * 256:(tb + 1) * 256], ALU.mult, ALU.add))
                return v.bn_stats(stats[:, bass.ds(unit * 6 + tb * 48, 6)], cols)

            def add_residuals(first, before, pairs):
                with dve.Fori(0, pairs) as it:
                    chain.loop(it, 6)
                    for n in range(2):
                        dve.wait_ge(evac_done, it * 2 + n + first + 1)
                        link(add_residual(n, 0, it * 2 + n))
                        mark(add_residual(n, 1, it * 2 + n), z_done, it * 2 + n + before + 3)
                    chain.end(pairs)

            def first_norm():
                for tb in range(TB):
                    mark(v.bn_aggr(mv[:, 2 * tb:2 * tb + 2], stats[:, tb * 48:(tb + 1) * 48]), lnv_done, tb + 1)
                dve.wait_ge(ln_in, 32)
                for tb in range(TB):
                    dve.wait_ge(lnr_done, tb + 1)
                    rows = h_tok[:, tb * D:(tb + 1) * D]
                    link(v.tensor_scalar(rows, rows, mv[:, 2 * tb:2 * tb + 1], rs[:, tb:tb + 1], ALU.subtract, ALU.mult))
                    link(v.tensor_tensor(rows, rows, ln_g, ALU.mult))
                    mark(v.tensor_tensor(rows, rows, ln_b, ALU.add), h_done, tb + 1)

            def second_norm():
                add_residuals(U_CO, UPM, UPM // 2 - 1)
                dve.wait_ge(evac_done, U_PQ - 1)
                link(add_residual(0, 0, UPM - 2))
                mark(add_residual(0, 1, UPM - 2), z_done, 2 * UPM + 1)
                for q in range(8):
                    tb, k4 = q // 4, q % 4
                    if k4 == 0:
                        if tb == 0:
                            dve.wait_ge(last0_sb, 1)
                        else:
                            dve.wait_ge(evac_done, U_PQ)
                        link(add_residual(1, tb, UPM - 1))
                        mark(v.bn_aggr(mv[:, 2 * tb:2 * tb + 2], stats[:, tb * 48:(tb + 1) * 48]), lnv_done, 3 + tb)
                        dve.wait_ge(lnr_done, 3 + tb)
                        link(v.reciprocal(rs[:, tb:tb + 1], mv[:, 2 * tb + 1:2 * tb + 2]))
                    cols = h_tok[:, tb * D + k4 * 512:tb * D + (k4 + 1) * 512]
                    mark(v.tensor_scalar(cols, cols, mv[:, 2 * tb:2 * tb + 1], rs[:, tb:tb + 1], ALU.subtract, ALU.mult),
                         unit_var, q + 1)
                    if q == 3:
                        dve.wait_ge(ln2c_in, 16)
                        for turned in (1, 3):
                            dve.wait_ge(tr_ps, 8 + turned + 1)
                            for k in range(4):
                                f = 4 * turned + k
                                ins = v.tensor_scalar(h_t[:, f * SEQ:f * SEQ + P], B[turned][:, k * P:(k + 1) * P],
                                                      ln2_g[:, f:f + 1], ln2_b[:, f:f + 1], ALU.mult, ALU.add)
                            ins.then_inc(tv_sb, 1)

            def first_rows_final():
                rows = h_tok[:, 0:D]
                dve.wait_ge(ln_in, 64)
                dve.wait_ge(tr_ps, 12)
                link(v.tensor_tensor(rows, rows, ln_g, ALU.mult))
                mark(v.tensor_tensor(rows, rows, ln_b, ALU.add), h_final[0], 1)

            dve.wait_ge(xtok_in, 16)
            add_residuals(U_MIX, 0, UPM // 2)
            first_norm()

            for m in range(MEM_HEADS):
                dve.wait_ge(cl_ps, m + 1)
                link(v.reduce_max(nmax2[:, 0:2], B[0].rearrange("p (b n) -> p b n", b=2), AX.X))
                mark(v.tensor_scalar(nmax[:, 0:2], nmax2[:, 0:2], -MEM_DH ** -0.5, None, ALU.mult), cl_rd, m + 1)
                dve.wait_ge(ce_done, 2 * m + 2)
                link(v.reciprocal(rec[:, 0:2], esum[:, 0:2]))
                for tb in range(TB):
                    cols = pc[:, tb * 256:(tb + 1) * 256]
                    mark(v.tensor_scalar(cols, cols, rec[:, tb:tb + 1], None, ALU.mult), cp_done, 2 * m + tb + 1)

            second_norm()

            def top16(vals, idx, src, rest):
                link(v.max(vals[:, 0:8], src))
                link(v.max_index(idx[:, 0:8], vals[:, 0:8], src))
                link(v.match_replace(rest, vals[:, 0:8], src, TAKEN))
                link(v.max(vals[:, 8:16], rest))
                link(v.max_index(idx[:, 8:16], vals[:, 8:16], rest))

            def experts_of(k, tb):
                return slice(tb * NE + k * PK, tb * NE + (k + 1) * PK)

            def choose(n):
                k, tb = n // 2, n % 2
                dve.wait_ge(psc_sb, n + 1 if n < 2 else k + 2)
                for g in (2 * tb, 2 * tb + 1):
                    top16(v16[:, g * PK:(g + 1) * PK], i16[:, g * PK:(g + 1) * PK], sc[:, g * P:(g + 1) * P],
                          sc2[:, g * P:(g + 1) * P])
                halves = i16f[:, 2 * tb * PK:2 * (tb + 1) * PK]
                link(v.tensor_copy(halves, i16[:, 2 * tb * PK:2 * (tb + 1) * PK]))
                cols = cand[:, tb * 256:(tb + 1) * 256]
                rows = v16[:, 2 * tb * PK:(2 * tb + 1) * PK].unsqueeze(2).to_broadcast([P, PK, PK])
                other = v16[:, (2 * tb + 1) * PK:(2 * tb + 2) * PK].unsqueeze(1).to_broadcast([P, PK, PK])
                link(v.tensor_tensor(cols.rearrange("p (a b) -> p a b", a=PK), rows, other, ALU.add))
                top16(top_s, pos, cols, cols)
                link(v.tensor_scalar(posh[:, 0:PK], pos, 4, None, ALU.logical_shift_right))
                link(v.tensor_scalar(posh[:, PK:2 * PK], pos, PK - 1, None, ALU.bitwise_and))
                link(v.tensor_copy(poshf, posh))
                link(v.tensor_tensor(eq.rearrange("p (r a) -> p r a", a=PK), poshf.unsqueeze(2).to_broadcast([P, 2 * PK, PK]),
                                     C[:, K_IOTA:K_IOTA + PK].unsqueeze(1).to_broadcast([P, 2 * PK, PK]), ALU.is_equal))
                eq4 = eq.rearrange("p (h r a) -> p h r a", h=2, a=PK)
                link(v.tensor_tensor(eq4, eq4, halves.rearrange("p (h a) -> p h a", h=2).unsqueeze(2).to_broadcast([P, 2, PK, PK]),
                                     ALU.mult))
                link(v.reduce_sum(idxh, eq.rearrange("p (r a) -> p r a", a=PK), AX.X))
                link(v.scalar_tensor_tensor(experts[:, experts_of(k, tb)], idxh[:, 0:PK], float(NKEYS), idxh[:, PK:2 * PK],
                                            ALU.mult, ALU.add))
                mark(v.tensor_tensor(e_top, top_s, top_s[:, 0:1].to_broadcast([P, PK]), ALU.subtract), tops_rd, n + 1)

            def weigh(n):
                dve.wait_ge(gexp_done, n + 1)
                link(v.reduce_sum(g2[:, 0:1], e_top, AX.X))
                link(v.reciprocal(g2[:, 0:1], g2[:, 0:1]))
                mark(v.tensor_tensor(gates[:, experts_of(n // 2, n % 2)], e_top, g2[:, 0:1].to_broadcast([P, PK]), ALU.mult), head_done, n + 1)

            def set_idx(b, par, fresh=False):
                if not fresh:
                    for e in range(BATCH):
                        dve.wait_ge(v_in[e], b * 16 - 16)
                        dve.wait_ge(u_in[e], b * 16 - 16)
                mark(v.tensor_copy(idx_fix[:, par * BATCH:(par + 1) * BATCH], experts[:, bass.ds(b * BATCH, BATCH)]), idx_set, b + 1)

            def products(b, tb, fresh=False):
                for e in range(BATCH):
                    if not fresh:
                        dve.wait_ge(gh_done, b * BATCH + e - BATCH + 1)
                    dve.wait_ge(u_in[e], b * 16 + 16)
                    mark(v.tensor_tensor_reduce(u_rows[e], u_rows[e], h_tok[:, tb * D:(tb + 1) * D], 1.0, 0.0, ALU.mult, ALU.add,
                                                dots[:, e:e + 1]), dot_done, b * BATCH + e + 1)

            def last_norm(tb, Y):
                if tb == 0:
                    dve.wait_ge(v_used, BPB * BATCH)
                for c in range(4):
                    if tb:
                        dve.wait_ge(bank_done, c + 1)
                    link(v.bn_stats(stats[:, c * 6:(c + 1) * 6], Y[c]))
                mark(v.bn_aggr(mv[:, 2 * tb:2 * tb + 2], stats[:, 0:24]), lnv_done, 5 + tb)
                dve.wait_ge(fin_in, 16 * 5)
                if tb:
                    dve.wait_ge(out_done, 16 * 4)
                for c in range(4):
                    cols = slice(c * 512, (c + 1) * 512)
                    link(v.scalar_tensor_tensor(fin_x[:, cols], Y[c], mv[:, 2 * tb:2 * tb + 1], fin_g[:, cols],
                                                ALU.subtract, ALU.mult))
                dve.wait_ge(lnr_done, 5 + tb)
                link(v.reciprocal(rs[:, tb:tb + 1], mv[:, 2 * tb + 1:2 * tb + 2]))
                for c in range(4):
                    cols = slice(c * 512, (c + 1) * 512)
                    mark(v.scalar_tensor_tensor(fin_x[:, cols], fin_x[:, cols], rs[:, tb:tb + 1], fin_b[c],
                                                ALU.mult, ALU.add), fin_done, 4 * tb + c + 1)

            choose(0)
            set_idx(0, 0, True)
            weigh(0)
            first_rows_final()
            for n in range(1, 2 * PEER_HEADS):
                choose(n)
                set_idx(n, n % 2, n == 1)
                weigh(n)
                products(n - 1, 0, n == 1)
            set_idx(EARLY + 1, 0)
            products(EARLY, 0)
            with dve.Fori((EARLY + 1) // 2, BPB // 2) as i:
                for n in range(2):
                    set_idx(i * 2 + n + 1, 1 - n)
                    products(i * 2 + n, 0)
            set_idx(BPB + 1, 1)
            dve.wait_ge(h_final[1], 1)
            products(BPB, 1)
            last_norm(0, B)
            with dve.Fori(BPB // 2, TB * BPB // 2 - 1) as i:
                for n in range(2):
                    set_idx(i * 2 + n + 2, n)
                    products(i * 2 + n + 1, 1)
            products(TB * BPB - 1, 1)
            last_norm(1, PJ)


def columns(a):
    return a.reshape(a.shape[0], KT, P).transpose(2, 1, 0).reshape(P, KT * a.shape[0])


def as_units(w):
    n = w.shape[1] // UN
    return w.reshape(KT, P, n, UN).transpose(2, 1, 0, 3).reshape(n, P, KT * UN)


def kernel(**inputs):
    import concourse.bacc as bacc
    from concourse.bass_utils import run_bass_kernel_spmd

    a = {k: np.ascontiguousarray(v) for k, v in inputs.items()}
    x, mem = a["x"][0], a["mem"][0]
    w_in = a["w_in"][0]

    def cut(at, j):
        return as_units(w_in[:, at + UN * j:at + UN * (j + 1)])[0]

    one = [as_units(a[n][0]) for n in ("w_branch_a", "w_branch_b", "w_mix_out", "w_ck", "w_cv", "w_cq", "w_co", "w_pq")]
    w_a, w_b, w_mix, w_ck, w_cv, w_cq, w_co, w_pq = one
    order = [cut(C_CKV, 0), cut(C_IK, 0)]
    for j in range(UPM):
        order += [cut(C_HF, j), cut(C_HQ, j), cut(C_HI, j), cut(C_HG, j)]
    order += list(w_ck)
    order += [cut(C_IQ, j) for j in range(UPM)]
    for j in range(UPM):
        order += [cut(C_GA, j), w_a[j]]
    for j in range(UPM):
        order += [cut(C_AQ, j), cut(C_GB, j)]
    order += list(w_b) + list(w_mix) + list(w_cv) + list(w_cq) + list(w_co) + list(w_pq)
    assert len(order) == UNITS

    def low_rank(w):
        return w.reshape(PAIRS, 2, 2, P, P).transpose(0, 3, 2, 1, 4).reshape(PAIRS, P, 512)

    arrays = {
        "x_tok": x.reshape(TB, P, D).transpose(1, 0, 2).reshape(P, TB * D),
        "x_cols": columns(x),
        "mem_cols": columns(mem),
        "units": np.stack(order),
        "const": constants(),
        "hits": bucket_hits(),
        "rel_bias": a["rel_bias"],
        "lb_logits": a["lb_logits"].reshape(2, HEADS, P).transpose(2, 0, 1).reshape(P, 2 * HEADS),
        "hg_norm": a["hg_norm_g"][0].reshape(HEADS, P).T,
        "ln2_cols": np.concatenate([a[n][0].reshape(KT, P).T for n in ("ln2_g", "ln2_b")], axis=1),
        "kv_g": a["kv_norm_g"][0],
        "ik_g": a["ik_norm_g"][0],
        "ik_b": a["ik_norm_b"][0],
        "w_ukv": np.concatenate([low_rank(a["w_uk"][0]), low_rank(a["w_uv"][0])], axis=2),
        "keys_cols": a["peer_keys"][0].reshape(2 * PEER_HEADS, NKEYS, P).transpose(2, 0, 1).reshape(P, 2 * PEER_HEADS * NKEYS),
        "ln_rows": np.concatenate([a[n] for n in ("ln1_g", "ln1_b", "ln2_g", "ln2_b", "ln3_g", "ln3_b")]),
        "peer_u": a["peer_u"][0],
        "peer_v": a["peer_v"][0],
    }
    arrays = {k: np.ascontiguousarray(v) for k, v in arrays.items()}
    nc = bacc.Bacc("TRN2", target_bir_lowering=False, num_devices=1)
    args = [nc.dram_tensor(n, v.shape, mybir.dt.from_np(v.dtype), kind="ExternalInput").ap() for n, v in arrays.items()]
    rb_scratch = nc.dram_tensor("rb_scratch", (HEADS, P, 384), F32, kind="Internal").ap()
    out = nc.dram_tensor("out", (TB, P, D), F32, kind="ExternalOutput").ap()
    trunk_layer(nc, *args, rb_scratch, out)
    r = run_bass_kernel_spmd(nc, [arrays], core_ids=[0])
    return r.results[0]["out"].reshape(1, SEQ, D)
```
